# Optimizing a Trainium2 kernel written in Bass

```python
import jax
import jax.numpy as jnp
from jax import lax
import numpy as np

D_MODEL = 1024
BATCH = 1
SEQ = 128
DEPTH = 2
DEC_BATCH = 1
DEC_SEQ = 1024
PAST_LEN = 128

GRID_W = 64
N_EVEN = (DEPTH + 1) // 2
N_ODD = DEPTH // 2
EPS = 1e-6
RET_HEADS = 4
RET_DK = 128
RET_DV = 128
RET_CHUNK = 128
ROPE_BASE = 10000.0
GMLP_GROUPS = 4
GMLP_CH = 128
GMLP_CHUNK = 128
AB_SPLITS = (RET_HEADS * RET_DK, RET_HEADS * RET_DK, RET_HEADS * RET_DV, RET_HEADS * RET_DV, GMLP_GROUPS * GMLP_CH, GMLP_GROUPS * GMLP_CH)
AB_IN = sum(AB_SPLITS)
AB_OUT = RET_HEADS * RET_DV + GMLP_GROUPS * GMLP_CH
D_RNN = D_MODEL
LRU_BLOCKS = 8
LRU_BS = D_RNN // LRU_BLOCKS
LRU_C = 8.0
CONV_W = 4
CONV_PAD_L = 2
CONV_PAD_R = 1
D_FF = 4 * D_MODEL

kernel_name = 'hybrid_retention_gmlp_rglru_dit_step'

def rmsnorm(x, g):
    xf = x.astype(jnp.float32)
    y = xf * lax.rsqrt(jnp.mean(xf * xf, axis=-1, keepdims=True) + EPS)
    return (y * g.astype(jnp.float32)).astype(x.dtype)

def to_heads(t, n_heads):
    b, l, _ = t.shape
    return t.reshape(b, l, n_heads, -1).transpose(0, 2, 1, 3)

def axial_rope(t):
    length = t.shape[2]
    pos = jnp.arange(length)
    row = (pos // GRID_W).astype(jnp.float32)
    col = (pos % GRID_W).astype(jnp.float32)
    half = t.shape[-1] // 2
    nf = half // 2
    inv_freq = ROPE_BASE ** (-jnp.arange(nf, dtype=jnp.float32) / nf)

    def rot(xa, p):
        ang = p[:, None] * inv_freq[None, :]
        cos, sin = jnp.cos(ang), jnp.sin(ang)
        x1, x2 = xa[..., :nf], xa[..., nf:]
        return jnp.concatenate([x1 * cos - x2 * sin, x1 * sin + x2 * cos], axis=-1)

    tf = t.astype(jnp.float32)
    return jnp.concatenate([rot(tf[..., :half], row), rot(tf[..., half:], col)], axis=-1)

def retention_dir(q, k, v, log_gamma, s0, exclusive):
    b, h, l, dk = q.shape
    dv = v.shape[-1]
    c = RET_CHUNK
    nc = l // c
    qc = q.reshape(b, h, nc, c, dk)
    kc = k.reshape(b, h, nc, c, dk)
    vc = v.reshape(b, h, nc, c, dv)
    i = jnp.arange(c, dtype=jnp.float32)
    off = 1.0 if exclusive else 0.0
    expo = i[:, None] - i[None, :] - off
    lg = log_gamma[:, None, None]
    intra_decay = jnp.where(expo >= 0.0, jnp.exp(lg * jnp.maximum(expo, 0.0)), 0.0)
    scores = jnp.einsum('bhncd,bhnjd->bhncj', qc, kc) * intra_decay[None, :, None]
    o = jnp.einsum('bhncj,bhnje->bhnce', scores, vc)
    k_decay = jnp.exp(log_gamma[:, None] * (c - 1.0 - i)[None, :])
    chunk_kv = jnp.einsum('bhnjd,bhnje->nbhde', kc * k_decay[None, :, None, :, None], vc)
    g_chunk = jnp.exp(log_gamma * c)[None, :, None, None]

    def step(s, kv):
        return g_chunk * s + kv, s

    s_final, s_prev = lax.scan(step, s0, chunk_kv)
    q_decay = jnp.exp(log_gamma[:, None] * (i + 1.0 - off)[None, :])
    o = o + jnp.einsum('bhncd,nbhde->bhnce', qc * q_decay[None, :, None, :, None], s_prev)
    return o.reshape(b, h, l, dv), s_final

def retention_bidir(q, k, v, gate, lg_f, lg_b, s0_f, s0_b):
    o_f, s_f = retention_dir(q, k, v, lg_f, s0_f, False)
    o_b, s_b = retention_dir(jnp.flip(q, 2), jnp.flip(k, 2), jnp.flip(v, 2), lg_b, s0_b, True)
    o = o_f + jnp.flip(o_b, 2)
    mu = jnp.mean(o, axis=-1, keepdims=True)
    var = jnp.mean(jnp.square(o - mu), axis=-1, keepdims=True)
    o = (o - mu) * lax.rsqrt(var + EPS)
    b, h, l, dv = o.shape
    o = o.transpose(0, 2, 1, 3).reshape(b, l, h * dv)
    return jax.nn.silu(gate.astype(jnp.float32)) * o, s_f, s_b

def chunk_gmlp(u, v, ws, bs):
    b, l, _ = u.shape
    nc = l // GMLP_CHUNK
    u = jax.nn.gelu(u.astype(jnp.float32))
    vf = jax.nn.gelu(v.astype(jnp.float32)).reshape(b, nc, GMLP_CHUNK, GMLP_GROUPS, GMLP_CH)
    vf = vf * lax.rsqrt(jnp.mean(vf * vf, axis=-1, keepdims=True) + EPS)
    s = jnp.einsum('gpq,bnqgc->bnpgc', ws.astype(jnp.float32), vf) + bs.astype(jnp.float32).T[None, None, :, :, None]
    return u * s.reshape(b, l, GMLP_GROUPS * GMLP_CH)

def centred_dwconv(x, w, bias):
    l = x.shape[1]
    xp = jnp.pad(x, ((0, 0), (CONV_PAD_L, CONV_PAD_R), (0, 0)))
    out = bias
    for j in range(CONV_W):
        out = out + xp[:, j:j + l, :] * w[j]
    return out

def block_diag_linear(x, w, bias):
    b, l, _ = x.shape
    y = jnp.einsum('blnc,ncd->blnd', x.reshape(b, l, LRU_BLOCKS, LRU_BS), w)
    return y.reshape(b, l, D_RNN) + bias

def linear_scan(a, bx, h0):
    def combine(e1, e2):
        a1, b1 = e1
        a2, b2 = e2
        return a1 * a2, a2 * b1 + b2

    a_cum, b_cum = lax.associative_scan(combine, (a, bx), axis=1)
    h = a_cum * h0[:, None, :] + b_cum
    return h, h[:, -1, :]

def rg_lru_dir(xc, wa, ba, wx, bx, lam, h0):
    r = jax.nn.sigmoid(block_diag_linear(xc, wa, ba))
    ig = jax.nn.sigmoid(block_diag_linear(xc, wx, bx))
    log_a = -LRU_C * r * jax.nn.softplus(-lam)
    a = jnp.exp(log_a)
    mult = jnp.sqrt(-jnp.expm1(2.0 * log_a))
    return linear_scan(a, mult * (ig * xc), h0)

def setup_inputs(seed: int = 0) -> dict:
    key = jax.random.key(seed)
    keys = list(jax.random.split(key, 40))

    def nrm(shape, scale):
        return scale * jax.random.normal(keys.pop(), shape, jnp.float32)

    f32 = jnp.float32
    ret_base = jnp.asarray(np.log(2.0 ** (5 + np.arange(RET_HEADS)) - 1.0), f32)
    a0 = jax.random.uniform(keys.pop(), (N_ODD, 2, D_RNN), f32, 0.9, 0.999)
    s0 = a0 ** (1.0 / LRU_C)
    return {
        'x_prompt': nrm((BATCH, SEQ, D_MODEL), 1.0),
        'x_sample': nrm((DEC_BATCH, DEC_SEQ, D_MODEL), 1.0),
        'c': nrm((DEC_BATCH, D_MODEL), 1.0),
        'c_ctx': nrm((D_MODEL,), 1.0),
        'state_ret_fwd': nrm((DEC_BATCH, N_EVEN, RET_HEADS, RET_DK, RET_DV), 0.3),
        'state_ret_bwd': nrm((DEC_BATCH, N_EVEN, RET_HEADS, RET_DK, RET_DV), 0.3),
        'state_lru_fwd': nrm((DEC_BATCH, N_ODD, D_RNN), 0.5),
        'state_lru_bwd': nrm((DEC_BATCH, N_ODD, D_RNN), 0.5),
        'mod_w': nrm((DEPTH, D_MODEL, 6 * D_MODEL), D_MODEL ** -0.5),
        'mod_b': nrm((DEPTH, 6 * D_MODEL), 0.01),
        'norm_mix': 1.0 + nrm((DEPTH, D_MODEL), 0.02),
        'norm_mlp': 1.0 + nrm((DEPTH, D_MODEL), 0.02),
        'mlp_w1': nrm((DEPTH, D_MODEL, D_FF), D_MODEL ** -0.5),
        'mlp_w2': nrm((DEPTH, D_FF, D_MODEL), D_FF ** -0.5),
        'ab_w_in': nrm((N_EVEN, D_MODEL, AB_IN), D_MODEL ** -0.5),
        'ab_w_out': nrm((N_EVEN, AB_OUT, D_MODEL), AB_OUT ** -0.5),
        'ret_decay_fwd': ret_base[None, :] + nrm((N_EVEN, RET_HEADS), 0.05),
        'ret_decay_bwd': ret_base[None, :] + nrm((N_EVEN, RET_HEADS), 0.05),
        'gmlp_ws': nrm((N_EVEN, GMLP_GROUPS, GMLP_CHUNK, GMLP_CHUNK), GMLP_CHUNK ** -0.5),
        'gmlp_bs': 1.0 + nrm((N_EVEN, GMLP_GROUPS, GMLP_CHUNK), 0.1),
        'lru_w_in': nrm((N_ODD, D_MODEL, 2 * D_RNN), D_MODEL ** -0.5),
        'lru_conv_w': nrm((N_ODD, CONV_W, D_RNN), CONV_W ** -0.5),
        'lru_conv_b': nrm((N_ODD, D_RNN), 0.01),
        'lru_gate_a_w': nrm((N_ODD, 2, LRU_BLOCKS, LRU_BS, LRU_BS), LRU_BS ** -0.5),
        'lru_gate_a_b': nrm((N_ODD, 2, D_RNN), 0.01),
        'lru_gate_x_w': nrm((N_ODD, 2, LRU_BLOCKS, LRU_BS, LRU_BS), LRU_BS ** -0.5),
        'lru_gate_x_b': nrm((N_ODD, 2, D_RNN), 0.01),
        'lru_lambda': jnp.log(s0) - jnp.log1p(-s0),
        'lru_w_out': nrm((N_ODD, D_RNN, D_MODEL), D_RNN ** -0.5),
        'final_norm': 1.0 + nrm((D_MODEL,), 0.02),
    }

def reference(x_prompt, x_sample, c, c_ctx, state_ret_fwd, state_ret_bwd, state_lru_fwd, state_lru_bwd,
              mod_w, mod_b, norm_mix, norm_mlp, mlp_w1, mlp_w2,
              ab_w_in, ab_w_out, ret_decay_fwd, ret_decay_bwd, gmlp_ws, gmlp_bs,
              lru_w_in, lru_conv_w, lru_conv_b, lru_gate_a_w, lru_gate_a_b, lru_gate_x_w, lru_gate_x_b,
              lru_lambda, lru_w_out, final_norm):
    f32 = jnp.float32
    ab_cuts = np.cumsum(AB_SPLITS)[:-1].tolist()

    def trunk(x, cond, ret_f0, ret_b0, lru_f0, lru_b0, latent):
        ret_f, ret_b, lru_f, lru_b = [], [], [], []
        for l in range(DEPTH):
            mod = (jax.nn.silu(cond.astype(f32)) @ mod_w[l].astype(f32) + mod_b[l].astype(f32))[:, None, :]
            sh1, sc1, g1, sh2, sc2, g2 = jnp.split(mod, 6, axis=-1)
            h = rmsnorm(x, norm_mix[l]).astype(f32) * (1.0 + sc1) + sh1
            if l % 2 == 0:
                e = l // 2
                q, k, v, g, u, vv = jnp.split(h @ ab_w_in[e].astype(f32), ab_cuts, axis=-1)
                q = to_heads(q, RET_HEADS)
                k = to_heads(k, RET_HEADS) * (RET_DK ** -0.5)
                v = to_heads(v, RET_HEADS)
                if latent:
                    q, k = axial_rope(q), axial_rope(k)
                o_ret, s_f, s_b = retention_bidir(
                    q, k, v, g,
                    jax.nn.log_sigmoid(ret_decay_fwd[e].astype(f32)),
                    jax.nn.log_sigmoid(ret_decay_bwd[e].astype(f32)),
                    ret_f0[:, e].astype(f32), ret_b0[:, e].astype(f32))
                o_gm = chunk_gmlp(u, vv, gmlp_ws[e], gmlp_bs[e])
                mix = jnp.concatenate([o_ret, o_gm], axis=-1) @ ab_w_out[e].astype(f32)
                ret_f.append(s_f)
                ret_b.append(s_b)
            else:
                o = l // 2
                gate_in, x_in = jnp.split(h @ lru_w_in[o].astype(f32), 2, axis=-1)
                xc = centred_dwconv(x_in, lru_conv_w[o].astype(f32), lru_conv_b[o].astype(f32))
                h_f, s_f = rg_lru_dir(xc, lru_gate_a_w[o, 0].astype(f32), lru_gate_a_b[o, 0].astype(f32),
                                      lru_gate_x_w[o, 0].astype(f32), lru_gate_x_b[o, 0].astype(f32),
                                      lru_lambda[o, 0].astype(f32), lru_f0[:, o].astype(f32))
                h_b, s_b = rg_lru_dir(jnp.flip(xc, 1), lru_gate_a_w[o, 1].astype(f32), lru_gate_a_b[o, 1].astype(f32),
                                      lru_gate_x_w[o, 1].astype(f32), lru_gate_x_b[o, 1].astype(f32),
                                      lru_lambda[o, 1].astype(f32), lru_b0[:, o].astype(f32))
                mix = (jax.nn.gelu(gate_in) * (h_f + jnp.flip(h_b, 1))) @ lru_w_out[o].astype(f32)
                lru_f.append(s_f)
                lru_b.append(s_b)
            x = x + (g1 * mix).astype(x.dtype)
            h = rmsnorm(x, norm_mlp[l]).astype(f32) * (1.0 + sc2) + sh2
            ff = jnp.square(jax.nn.relu(h @ mlp_w1[l].astype(f32))) @ mlp_w2[l].astype(f32)
            x = x + (g2 * ff).astype(x.dtype)
        y = rmsnorm(x, final_norm)
        return y, jnp.stack(ret_f, axis=1), jnp.stack(ret_b, axis=1), jnp.stack(lru_f, axis=1), jnp.stack(lru_b, axis=1)

    bp = x_prompt.shape[0]
    zero_ret = jnp.zeros((bp, N_EVEN, RET_HEADS, RET_DK, RET_DV), f32)
    zero_lru = jnp.zeros((bp, N_ODD, D_RNN), f32)
    y_prompt, new_ret_fwd, new_ret_bwd, new_lru_fwd, new_lru_bwd = trunk(
        x_prompt, c_ctx[None, :], zero_ret, zero_ret, zero_lru, zero_lru, False)

    y_sample = trunk(x_sample, c, state_ret_fwd, state_ret_bwd, state_lru_fwd, state_lru_bwd, True)[0]

    return (y_prompt, y_sample, new_ret_fwd, new_ret_bwd, new_lru_fwd, new_lru_bwd)


_drawn_inputs = setup_inputs


def setup_inputs(seed=0):
    import zlib

    import numpy as np

    out = dict(_drawn_inputs(seed))
    spreads = {}
    factors = {'state_ret_fwd': 17.697,
     'state_ret_bwd': 16.827,
     'state_lru_fwd': 10.744,
     'state_lru_bwd': 11.884,
     'norm_mlp': 3.297,
     'lru_conv_b': 3.758,
     'lru_gate_a_b': 41.792,
     'lru_gate_x_b': 26.639,
     'final_norm': 23.162,
     'norm_mix': 3.048}
    for name, (base, spread) in spreads.items():
        noise = np.random.default_rng([zlib.crc32(name.encode()), seed]).standard_normal(out[name].shape)
        drawn = base * np.exp(spread * noise) if base else spread * noise
        out[name] = jnp.asarray(drawn.astype(out[name].dtype))
    for name, factor in factors.items():
        out[name] = (out[name] * factor).astype(out[name].dtype)
    return out
```

```python
from contextlib import ExitStack

import numpy as np

import concourse.bass as bass
from concourse import mybir

F32 = mybir.dt.float32
F32R = mybir.dt.float32r
ALU = mybir.AluOpType
ACT = mybir.ActivationFunctionType
ds = bass.ds

P = 128
D_MODEL = 1024
LAT = 1024
CTX = 128
TOK = LAT + CTX
BANKS = 3
CH = TOK // BANKS
NCH = TOK // P
LCH = LAT // P
KT = D_MODEL // P
D_FF = 4 * D_MODEL
HEADS = 4
HD = HEADS * P
LRU_C = 8.0
EPS = 1e-6
GRID_W = 64
ROPE_BASE = 10000.0
GRP = 4
GROUPS = D_FF // P // GRP
MODS = 6 * KT
SH1, SC1, G1, SH2, SC2, G2 = (n * KT for n in range(6))

SECTIONS = (1, 2, 0, 3, 5, 4)

R_MODB, R_NMIX, R_NMLP = 0, 96, 112
R_CONVW, R_CONVB, R_GA, R_GX, R_LAM, R_LF, R_LB, R_FN, R_C = (
    128 + n for n in (0, 32, 40, 56, 72, 88, 96, 104, 112))

C_ID, C_DF, C_DB, C_MF, C_MB, C_QF, C_QB, C_KF, C_KB = 0, 128, 256, 384, 512, 640, 768, 896, 897
C_ALL = 898

HEAD_UNITS, HEAD_ITEMS, HEAD_MINIS, HEAD_MODS = 6, 16, 10, 8
BLK_UNITS, BLK_ITEMS, BLK_MINIS = 2, 6, 4
GRP_UNITS, GRP_ITEMS, GRP_MINIS, GRP_MODS = 8, 12, 4, 6

START_ITEMS = 10
FIRST_MODS = 2 * KT


class Place:

    def __init__(self, units, items, minis):
        self.units, self.items, self.minis = units, items, minis

    def after(self, units, items, minis):
        return Place(self.units + units, self.items + items, self.minis + minis)


AT_NORM = [None] * 5
AT_MIX = [None] * 2
AT_OUT = [None] * 2
AT_MLP = [None] * 2
AT_NORM[0] = Place(0, START_ITEMS, START_ITEMS)
AT_MIX[0] = AT_NORM[0].after(0, 1, 1)
AT_OUT[0] = AT_MIX[0].after(HEADS * HEAD_UNITS, HEADS * HEAD_ITEMS, HEADS * HEAD_MINIS)
AT_NORM[1] = AT_OUT[0].after(KT, KT, 0)
AT_MLP[0] = AT_NORM[1].after(0, 1, 1)
AT_NORM[2] = AT_MLP[0].after(GROUPS * GRP_UNITS, GROUPS * GRP_ITEMS, GROUPS * GRP_MINIS)
AT_MIX[1] = AT_NORM[2].after(0, 1, 1)
AT_OUT[1] = AT_MIX[1].after(KT * BLK_UNITS, KT * BLK_ITEMS, KT * BLK_MINIS)
AT_NORM[3] = AT_OUT[1].after(KT, KT, 0)
AT_MLP[1] = AT_NORM[3].after(0, 1, 1)
AT_NORM[4] = AT_MLP[1].after(GROUPS * GRP_UNITS, GROUPS * GRP_ITEMS, GROUPS * GRP_MINIS)
AT_END = AT_NORM[4].after(0, 1, 1)
UNITS = AT_END.units


class Steps:

    def __init__(self):
        self.base, self.n, self.loop, self.per = 0, 0, None, 0

    def enter(self, loop, per):
        self.base, self.n, self.loop, self.per = self.base + self.n, 0, loop, per

    def leave(self, times):
        assert self.n == self.per, f"a loop's iteration has {self.n} steps, not {self.per}"
        self.base, self.n, self.loop = self.base + times * self.per, 0, None

    def done(self):
        self.n += 1
        return self.base + self.n if self.loop is None else self.loop * self.per + (self.base + self.n)


def build(nc, a):
    with ExitStack() as ctx:
        here = [(nc.sbuf_base + 31) // 32 * 32]

        def region(size):
            at = here[0]
            here[0] += (size + 31) // 32 * 32
            assert here[0] <= nc.sbuf_usable_end, f"{here[0]} of {nc.sbuf_usable_end} bytes"
            return at

        def sb(name, shape, at=None, dtype=F32):
            size = 4 * int(np.prod(shape))
            return nc.alloc_sbuf_tensor_at(name, [P] + list(shape), dtype, offset=region(size) if at is None else at)

        TB = 4 * TOK
        x_at = region(KT * TB)
        x = sb("x", [KT, TOK], x_at)
        mix = sb("mix", [KT, TOK], x_at)
        h_at = region(2 * KT * TB)
        h_hi = sb("h_hi", [KT, TOK], h_at, F32R)
        h_lo = sb("h_lo", [KT, TOK], h_at + KT * TB, F32R)
        x_rows = sb("x_rows", [NCH, D_MODEL], h_at)
        y_cols = sb("y_cols", [KT, TOK], h_at)
        y_rows = sb("y_rows", [NCH, D_MODEL], h_at + KT * TB)
        w_raw = sb("w_raw", [2, D_MODEL])
        w_hi = sb("w_hi", [2, D_MODEL], None, F32R)
        w_lo = sb("w_lo", [2, D_MODEL], None, F32R)
        mod_raw = sb("mod_raw", [2, KT, P])
        t_at = [region(TB) for _ in range(10)]
        tables_at = region(4 * 2 * LAT)

        def tile_at(n, name, dtype=F32):
            return sb(name, [TOK], t_at[n], dtype)

        turned = tile_at(0, "turned")
        swapped = tile_at(1, "swapped")
        kT = tile_at(2, "kT")
        v_raw = tile_at(3, "v_raw")
        k_fwd = tile_at(4, "k_fwd")
        k_bwd = tile_at(5, "k_bwd")
        qT = tile_at(6, "qT")
        v_row = tile_at(7, "v_row")
        probs = tile_at(8, "probs")
        s_bwd = tile_at(9, "s_bwd")
        rope = sb("rope", [2, LAT], tables_at)
        sumsq = tile_at(8, "sumsq")
        square_0 = tile_at(9, "square_0")
        square_1 = sb("square_1", [TOK], tables_at)
        square_1_first = tile_at(0, "square_1_first")
        rstd = tile_at(1, "rstd")
        scaled = [tile_at(2, "scaled_0"), tile_at(3, "scaled_1")]
        modulated = [tile_at(4, "modulated_0"), tile_at(5, "modulated_1")]
        hid_hi = sb("hid_hi", [GRP, TOK], t_at[0], F32R)
        hid_lo = sb("hid_lo", [GRP, TOK], t_at[4], F32R)
        relu = sb("relu", [TOK], tables_at)
        relu2 = tile_at(9, "relu2")
        xc = tile_at(0, "xc")
        rate = [tile_at(1, "rate_f"), tile_at(3, "rate_b")]
        gated = [tile_at(2, "gated_f"), tile_at(4, "gated_b")]
        gelu_gate = tile_at(5, "gelu_gate")
        denom = [tile_at(6, "denom_f"), tile_at(8, "denom_b")]
        root = [tile_at(7, "root_f"), tile_at(9, "root_b")]
        LPAD, RPAD = 2, 1
        CTX0 = LPAD + LAT + RPAD
        xin = sb("xin", [CTX0 + LPAD + CTX + RPAD], tables_at)
        gate_w = sb("gate_w", [4, P], tables_at + 4 * 1160)
        par_rows = sb("par_rows", [2, P], t_at[0])
        ws_rows = sb("ws_rows", [HEADS, P], t_at[1])
        consts = sb("consts", [C_ALL], t_at[2])
        dec_row = sb("dec_row", [2 * HEADS], t_at[3])
        bs_row = sb("bs_row", [HEADS * P], t_at[4])
        exps = sb("exps", [2, HEADS, P], t_at[5])
        sp_z, sp_neg, sp_max, sp_exp, sp_r, sp_r2, sp_q = (
            sb(name, [24], t_at[6] + 128 * n) for n, name in enumerate(
                ("sp_z", "sp_neg", "sp_max", "sp_exp", "sp_r", "sp_r2", "sp_q")))
        ident = sb("ident", [P])
        ones = sb("ones", [P])
        mask = sb("mask", [HEADS, P])
        q_dec = sb("q_dec", [2, HEADS, P])
        bs_all = sb("bs_all", [HEADS, P])
        wsT = sb("wsT", [HEADS, P])
        par = sb("par", [2 * P])
        cond = sb("cond", [2, KT])
        mod = sb("mod", [2, MODS, 2])
        gain = sb("gain", [KT, 2])
        k_dec = sb("k_dec", [2, HEADS])
        g_chunk = sb("g_chunk", [2, HEADS])
        lg = sb("lg", [2 * HEADS])
        lru_rate = sb("lru_rate", [2 * KT])
        eps = sb("eps", [1])
        s0_fwd = sb("s0_fwd", [P])
        stats = sb("stats", [NCH, 6])
        mean_var = sb("mean_var", [NCH, 2])
        row_rstd = sb("row_rstd", [NCH])
        vf_sum = sb("vf_sum", [NCH])
        vf_rstd = sb("vf_rstd", [NCH])
        lru_last = sb("lru_last", [2, KT])

        psum = ctx.enter_context(nc.psum_tensor("psum", [P, 2, BANKS, 512], F32))
        mod_psum = ctx.enter_context(nc.psum_tensor("mod_psum", [P, 512], F32))
        x_spill = nc.dram_tensor("x_spill", (P, KT * TOK), F32, kind="Internal").ap()

        def sem(name):
            return ctx.enter_context(nc.semaphore(name))

        raw_landed = [sem("raw_landed_0"), sem("raw_landed_1")]
        hi_done = sem("hi_done")
        split_done = sem("split_done")
        unit_done = sem("unit_done")
        mini_done = sem("mini_done")
        read_out = [sem("read_out_0"), sem("read_out_1")]
        mod_landed = [sem("mod_landed_0"), sem("mod_landed_1")]
        mod_used = sem("mod_used")
        mod_read = sem("mod_read")
        par_landed = sem("par_landed")
        x_landed = sem("x_landed")
        ones_set = sem("ones_set")
        cond_ready = sem("cond_ready")
        neg_abs_ready = sem("neg_abs_ready")
        exp_ready = sem("exp_ready")
        decays_ready = sem("decays_ready")
        powers_ready = sem("powers_ready")
        gain_ready = sem("gain_ready")
        sq_ready = sem("sq_ready")
        sq_added = sem("sq_added")
        scaled_ready = sem("scaled_ready")
        part_hi = sem("part_hi")
        h_ready = sem("h_ready")
        x_spilled = sem("x_spilled")
        x_back = sem("x_back")
        projected = sem("projected")
        k_ready = sem("k_ready")
        q_ready = sem("q_ready")
        o_var = sem("o_var")
        o_root = sem("o_root")
        o_ready = sem("o_ready")
        vf_root = sem("vf_root")
        vf_ready = sem("vf_ready")
        gm_out = sem("gm_out")
        state_in = sem("state_in")
        state_out = sem("state_out")
        relu2_ready = sem("relu2_ready")
        hid_part_hi = sem("hid_part_hi")
        hid_ready = sem("hid_ready")
        xc_ready = sem("xc_ready")
        gate_landed = sem("gate_landed")
        tanh_ready = sem("tanh_ready")
        root_ready = sem("root_ready")
        lru_done = sem("lru_done")
        y_ready = sem("y_ready")
        stored = sem("stored")
        passed = sem("passed")
        act_step = sem("act_step")
        dve_step = sem("dve_step")

        def by_bank(t):
            return t.rearrange("p (c t) -> p c t", c=BANKS)

        def whole(s):
            return psum[:, s, :, 0:CH]

        def part(s, n):
            return psum[:, s, n // 3, n % 3 * P:(n % 3 + 1) * P]

        def chunk(t, n):
            return t[:, n * P:(n + 1) * P]

        def tile_of(t, k):
            return t[:, k, :] if isinstance(k, int) else t[:, ds(k, 1), :].rearrange("p a t -> p (a t)")

        def col(t, n):
            return t[:, n:n + 1] if isinstance(n, int) else t[:, ds(n, 1)]

        def at(i, per, c):
            return c if i is None else i * per + c

        LATC = LAT // CH
        LREST = LAT - LATC * CH

        def pieces(s, t):
            return (
                (psum[:, s, 0:LATC, 0:CH], t[:, 0:LATC * CH].rearrange("p (c t) -> p c t", c=LATC), 0),
                (psum[:, s, LATC, 0:LREST], t[:, LATC * CH:LAT], 0),
                (psum[:, s, LATC, LREST:CH], t[:, LAT:TOK], 1),
            )

        def item_out(eng, i, per, c):
            eng.wait_ge(read_out[c % 2], at(i, per // 2, c // 2 + 2))

        def square(n, k):
            return square_0 if k % 2 == 0 else square_1 if n else square_1_first

        par_loads = [(par_rows[r % P:r % P + n, r // P, :], src) for r, n, src in (
            (R_MODB, 2 * MODS, a["mod_b"].rearrange("l (m p) -> (l m) p", p=P)),
            (R_NMIX, 2 * KT, a["norm_mix"].rearrange("l (m p) -> (l m) p", p=P)),
            (R_NMLP, 2 * KT, a["norm_mlp"].rearrange("l (m p) -> (l m) p", p=P)),
            (R_CONVW, 4 * KT, a["lru_conv_w"][0].rearrange("j (m p) -> (j m) p", p=P)),
            (R_CONVB, KT, a["lru_conv_b"][0].rearrange("(m p) -> m p", p=P)),
            (R_GA, 2 * KT, a["lru_gate_a_b"][0].rearrange("j (m p) -> (j m) p", p=P)),
            (R_GX, 2 * KT, a["lru_gate_x_b"][0].rearrange("j (m p) -> (j m) p", p=P)),
            (R_LAM, 2 * KT, a["lru_lambda"][0].rearrange("j (m p) -> (j m) p", p=P)),
            (R_LF, KT, a["state_lru_fwd"][0].rearrange("l (m p) -> (l m) p", p=P)),
            (R_LB, KT, a["state_lru_bwd"][0].rearrange("l (m p) -> (l m) p", p=P)),
            (R_FN, KT, a["final_norm"].rearrange("(m p) -> m p", p=P)),
            (R_C, KT, a["c"][0].rearrange("(m p) -> m p", p=P)),
            (R_C + KT, KT, a["c_ctx"].rearrange("(m p) -> m p", p=P)),
        )]
        par_loads += [
            (consts[:], a["consts"]), (rope[:], a["rope"]),
            (ws_rows[:], a["gmlp_ws"][0].rearrange("g p q -> p g q")),
            (dec_row[0:1, 0:HEADS], a["ret_decay_fwd"]), (dec_row[0:1, HEADS:2 * HEADS], a["ret_decay_bwd"]),
            (bs_row[0:1, :], a["gmlp_bs"].rearrange("e g p -> e (g p)")),
        ]
        N_PAR = len(par_loads)

        block = ctx.enter_context(nc.Block())

        @block.sync
        def _(sp):
            sp.nop().then_inc(state_out, 32)
            for n in range(NCH):
                src = a["x_sample"][0, n * P:(n + 1) * P, :] if n < LCH else a["x_prompt"][0]
                sp.dma_start(x_rows[:, n, :], src).then_inc(x_landed, 16)

            def load_unit(i, per, c, src):
                sp.wait_ge(split_done, at(i, per, c + 1))
                sp.sem_inc(passed, 1)
                dst = w_raw[:, c % 2, :].rearrange("p (k m) -> p k m", k=src.shape[1])
                sp.dma_start(dst, src).then_inc(raw_landed[c % 2], 16)

            def load_mod(i, per, c, layer):
                src = cols(a["mod_w"][layer], at(i, per, c - layer * MODS) * P)
                sp.wait_ge(mod_used, at(i, per, c + 1))
                sp.dma_start(mod_raw[:, c % 2], src).then_inc(mod_landed[c % 2], 16)

            def cols(w, start):
                w = w[:, start:start + P] if isinstance(start, int) else w[:, ds(sp.snap(start), P)]
                return w.rearrange("(k p) m -> p k m", p=P)

            def out_proj(l, w):
                for c in range(KT):
                    load_unit(None, 0, AT_OUT[l].units + c, cols(w, c * P))
                    if c == 1:
                        sp.wait_ge(h_ready, (3 * l + 2) * KT)
                        sp.dma_start(x[:].rearrange("p k t -> p (k t)"), x_spill).then_inc(x_back, 16)

            def mlp(l):
                u = AT_MLP[l].units
                with sp.Fori(0, GROUPS) as g:
                    for j in range(GRP):
                        load_unit(g, GRP_UNITS, u + j, cols(a["mlp_w1"][l], g * (GRP * P) + j * P))
                        if l == 0:
                            load_mod(g, GRP_MODS, MODS + j, 1)
                    for j in range(GRP):
                        src = a["mlp_w2"][l][ds(sp.snap(g * (GRP * P)), GRP * P), j * 2 * P:(j + 1) * 2 * P]
                        load_unit(g, GRP_UNITS, u + GRP + j, src.rearrange("(k p) m -> p k m", p=P))
                        if l == 0 and GRP + j < GRP_MODS:
                            load_mod(g, GRP_MODS, MODS + GRP + j, 1)

            def spill(l):
                sp.wait_ge(h_ready, (3 * l + 1) * KT)
                sp.dma_start(x_spill, x[:].rearrange("p k t -> p (k t)")).then_inc(x_spilled, 16)

            for m in range(FIRST_MODS):
                load_mod(None, 0, m, 0)
            spill(0)

            with sp.Fori(0, HEADS) as h:
                for j, section in enumerate(SECTIONS):
                    load_unit(h, HEAD_UNITS, j, cols(a["ab_w_in"][0], h * P + section * HD))
                    if j == 1:
                        sp.wait_ge(unit_done, h * HEAD_UNITS + 1)
                        sp.dma_start(s0_fwd[:], a["state_ret_fwd"][0, 0, ds(h, 1)].rearrange("a d e -> (a d) e")).then_inc(state_in, 16)
                        sp.dma_start(chunk(s_bwd, LCH - 1), a["state_ret_bwd"][0, 0, ds(h, 1)].rearrange("a d e -> (a d) e")).then_inc(state_in, 16)
                    load_mod(h, HEAD_MODS, FIRST_MODS + j, 0)
                    if j == 5:
                        load_mod(h, HEAD_MODS, FIRST_MODS + 6, 0)
                        load_mod(h, HEAD_MODS, FIRST_MODS + 7, 0)
                item_out(sp, h, HEAD_ITEMS, AT_MIX[0].items + 6)
                sp.dma_start(a["new_ret_bwd"][0, 0, ds(h, 1)].rearrange("a d e -> (a d) e"), chunk(s_bwd, LCH)).then_inc(state_out, 16)
                item_out(sp, h, HEAD_ITEMS, AT_MIX[0].items + 9)
                sp.dma_start(a["new_ret_fwd"][0, 0, ds(h, 1)].rearrange("a d e -> (a d) e"), chunk(k_bwd, LCH)).then_inc(state_out, 16)
            out_proj(0, a["ab_w_out"][0])
            mlp(0)
            spill(1)

            with sp.Fori(0, KT) as b:
                load_unit(b, BLK_UNITS, AT_MIX[1].units, cols(a["lru_w_in"][0], b * P + D_MODEL))
                load_unit(b, BLK_UNITS, AT_MIX[1].units + 1, cols(a["lru_w_in"][0], b * P))
                sp.wait_ge(mini_done, at(b, BLK_MINIS, AT_MIX[1].minis))
                for d in range(2):
                    for j, name in enumerate(("lru_gate_a_w", "lru_gate_x_w")):
                        src = a[name][0, d, ds(b, 1)].rearrange("a c d -> (a c) d")
                        sp.dma_start(gate_w[:, 2 * d + j, :], src).then_inc(gate_landed, 16)
            out_proj(1, a["lru_w_out"][0])
            mlp(1)

            sp.wait_ge(lru_done, 1 + KT)
            sp.dma_start(a["new_lru_fwd"][0, 0].rearrange("(b p) -> p b", p=P), lru_last[:, 0, :]).then_inc(stored, 16)
            sp.dma_start(a["new_lru_bwd"][0, 0].rearrange("(b p) -> p b", p=P), lru_last[:, 1, :]).then_inc(stored, 16)
            for n in range(NCH):
                item_out(sp, None, 0, AT_END.items + n)
                dst = a["y_sample"][0, n * P:(n + 1) * P, :] if n < LCH else a["y_prompt"][0]
                sp.dma_start(dst, y_rows[:, n, :]).then_inc(stored, 16)
            sp.wait_ge(stored, 16 * (NCH + 2))
            sp.wait_ge(state_out, 32 + 32 * HEADS)
            sp.wait_ge(x_spilled, 32)

        @block.gpsimd
        def _(pool):
            pool.nop().then_inc(split_done, 2)
            pool.memset(ones[:], 1.0).then_inc(ones_set, 1)
            pool.memset(eps[:], EPS).then_inc(ones_set, 1)

            def split(i, s):
                pool.wait_ge(raw_landed[s], at(i, 16, 16))
                if i is not None:
                    pool.wait_ge(unit_done, i * 2 + (s - 1))
                pool.sem_inc(passed, 1)
                pool.tensor_copy(w_hi[:, s, :], w_raw[:, s, :]).then_inc(hi_done, 1)
                pool.wait_ge(hi_done, at(i, 2, s + 1))
                pool.tensor_tensor(w_lo[:, s, :], w_raw[:, s, :], w_hi[:, s, :].bitcast(F32), ALU.subtract).then_inc(split_done, 1)

            split(None, 0)
            split(None, 1)
            with pool.Fori(1, UNITS // 2) as i:
                split(i, 0)
                split(i, 1)

        @block.tensor
        def _(pe):
            pe.nop().then_inc(read_out[0], 1)
            pe.nop().then_inc(read_out[1], 1)
            pe.nop().then_inc(mod_used, 2)

            def take_set(i, per, c):
                pe.wait_ge(read_out[c % 2], at(i, per // 2, c // 2 + 1))
                return c % 2

            def three_passes(s, hi, lo, in_hi, in_lo, tile_wait=None):
                for k in range(len(hi)):
                    if tile_wait:
                        tile_wait(k)
                    for w, v in ((hi[k], in_hi), (hi[k], in_lo), (lo[k], in_hi)):
                        for c in range(BANKS):
                            last = pe.matmul(psum[:, s, c, 0:CH], w, v[:, k, c * CH:(c + 1) * CH],
                                             start=(k == 0 and w is hi[k] and v is in_hi),
                                             stop=(k == len(hi) - 1 and w is lo[k]))
                return last

            def parts(w, c, n, start=0):
                view = w[:, c % 2, :].rearrange("p (k m) -> p k m", k=n)
                return [view[:, k, start:start + P] for k in range(n)]

            def project(i, items, item, per, unit):
                s = take_set(i, items, item)
                pe.wait_ge(split_done, at(i, per, unit + 3))
                return three_passes(s, parts(w_hi, unit, KT), parts(w_lo, unit, KT), h_hi, h_lo)

            def modulate(i, per, c, psum_col):
                pe.wait_ge(mod_landed[c % 2], at(i, 16 * (per // 2), 16 * (c // 2 + 1)))
                start = psum_col * 2
                dst = mod_psum[:, start:start + 2] if i is None else mod_psum[:, ds(start, 2)]
                for k in range(KT):
                    last = pe.matmul(dst, mod_raw[:, c % 2, k, :], cond[:, :, k], start=(k == 0), stop=(k == KT - 1))
                last.then_inc(mod_used, 1)

            def turn(s, t, n_of=NCH):
                for n in range(n_of):
                    last = pe.transpose(part(s, n), chunk(t, n), ident[:])
                return last

            def norm(n):
                s = take_set(None, 0, AT_NORM[n].items)
                pe.wait_ge(sq_added, (KT - 1) * (n + 1))
                for c in range(BANKS):
                    last = pe.matmul(psum[:, s, c, 0:CH], ones[:], sumsq[:, c * CH:(c + 1) * CH], start=True, stop=True)
                last.then_inc(mini_done, 1)

            pe.wait_ge(ones_set, 2)
            pe.wait_ge(par_landed, 16 * N_PAR)
            s = take_set(None, 0, 0)
            for n in range(2):
                pe.transpose(psum[:, s, 0, n * P:(n + 1) * P], par_rows[:, n, :], consts[:, C_ID:C_ID + P])
            for n in range(HEADS):
                pe.transpose(psum[:, s, 1 + n // 2, n % 2 * P:(n % 2 + 1) * P], ws_rows[:, n, :], consts[:, C_ID:C_ID + P])
            pe.matmul(psum[:, s, 0, 2 * P:2 * P + 2 * HEADS], ones[0:1, :], dec_row[0:1, :], start=True, stop=True)
            for n in range(2):
                last = pe.matmul(psum[:, s, 1 + n, 2 * P:4 * P], ones[0:1, :], bs_row[0:1, n * 2 * P:(n + 1) * 2 * P],
                                 start=True, stop=True)
            last.then_inc(mini_done, 1)
            for n in range(NCH):
                s = take_set(None, 0, 1 + n)
                if n == 0:
                    pe.wait_ge(x_landed, 16 * NCH)
                for k in range(KT):
                    last = pe.transpose(psum[:, s, k // 4, k % 4 * P:(k % 4 + 1) * P], x_rows[:, n, k * P:(k + 1) * P],
                                        consts[:, C_ID:C_ID + P])
                last.then_inc(mini_done, 1)
            pe.wait_ge(cond_ready, 1)
            for m in range(FIRST_MODS):
                modulate(None, 0, m, m)
            norm(0)

            pe.wait_ge(h_ready, KT)
            I0, U0, M0 = AT_MIX[0].items, AT_MIX[0].units, FIRST_MODS
            with pe.Fori(0, HEADS) as h:
                def big(item, unit):
                    return project(h, HEAD_ITEMS, I0 + item, HEAD_UNITS, U0 + unit)

                def mini(item):
                    return take_set(h, HEAD_ITEMS, I0 + item)

                def mods(c):
                    modulate(h, HEAD_MODS, M0 + c, h * HEAD_MODS + (FIRST_MODS + c))

                big(0, 0).then_inc(unit_done, 1)
                pe.wait_ge(mod_read, h + 1)
                mods(0)
                big(1, 1).then_inc(unit_done, 1)
                mods(1)
                s = mini(2)
                pe.wait_ge(k_ready, h + 1)
                turn(s, kT).then_inc(mini_done, 1)
                big(3, 2).then_inc(unit_done, 1)
                mods(2)
                s = mini(4)
                item_out(pe, h, HEAD_ITEMS, I0 + 1)
                turn(s, v_raw).then_inc(mini_done, 1)
                big(5, 3).then_inc(unit_done, 1)
                mods(3)
                s = mini(6)
                for n in range(NCH):
                    last = pe.matmul(part(s, n), chunk(k_bwd, n), chunk(v_row, n), start=True, stop=True)
                last.then_inc(mini_done, 1)
                s = mini(7)
                pe.wait_ge(q_ready, h + 1)
                for n in range(NCH):
                    last = pe.matmul(part(s, n), chunk(kT, n), chunk(qT, n), start=True, stop=True)
                last.then_inc(mini_done, 1)
                big(8, 4).then_inc(unit_done, 1)
                mods(4)
                s = mini(9)
                for n in range(NCH):
                    last = pe.matmul(part(s, n), chunk(k_fwd, n), chunk(v_row, n), start=True, stop=True)
                last.then_inc(mini_done, 1)
                s = mini(10)
                item_out(pe, h, HEAD_ITEMS, I0 + 5)
                turn(s, v_raw).then_inc(mini_done, 1)
                big(11, 5).then_inc(unit_done, 1)
                mods(5)
                mods(6)
                mods(7)
                s = mini(12)
                item_out(pe, h, HEAD_ITEMS, I0 + 9)
                for n in range(NCH):
                    last = pe.matmul(part(s, n), chunk(probs, n), chunk(v_row, n), start=True, stop=(n == LCH))
                    if n < LCH:
                        state = s0_fwd[:] if n == 0 else chunk(k_bwd, n)
                        pe.matmul(part(s, n), chunk(turned, n), state, start=False, stop=False)
                        last = pe.matmul(part(s, n), chunk(swapped, n), chunk(s_bwd, n), start=False, stop=True)
                last.then_inc(mini_done, 1)
                s = mini(13)
                item_out(pe, h, HEAD_ITEMS, I0 + 8)
                turn(s, kT).then_inc(mini_done, 1)
                s = mini(14)
                pe.wait_ge(o_ready, h + 1)
                turn(s, v_raw).then_inc(mini_done, 1)
                s = mini(15)
                pe.wait_ge(vf_ready, h + 1)
                for n in range(NCH):
                    last = pe.matmul(part(s, n), chunk(kT, n), tile_of(wsT, h), start=True, stop=True)
                last.then_inc(mini_done, 1)

            def out_proj(l):
                pe.wait_ge(h_ready, (3 * l + 2) * KT)
                for c in range(KT):
                    project(None, 0, AT_OUT[l].items + c, 0, AT_OUT[l].units + c).then_inc(unit_done, 1)

            def mlp(l):
                I, U = AT_MLP[l].items, AT_MLP[l].units
                pe.wait_ge(h_ready, (3 * l + 3) * KT)
                with pe.Fori(0, GROUPS) as g:
                    def mods(c):
                        if l == 0 and c < GRP_MODS:
                            if c == 0:
                                pe.wait_ge(mod_read, g + (1 + HEADS))
                            modulate(g, GRP_MODS, MODS + c, g * GRP_MODS + (MODS + c))

                    for j in range(GRP):
                        project(g, GRP_ITEMS, I + j, GRP_UNITS, U + j).then_inc(unit_done, 1)
                        mods(j)

                    def hidden(k):
                        if k in (0, GRP - 1):
                            pe.wait_ge(hid_ready, at(g, BANKS * GRP, BANKS * (GRP * GROUPS * l + (GRP if k else GRP - 1)) + 1))

                    for j in range(GRP):
                        unit = U + GRP + j
                        for half in range(2):
                            s = take_set(g, GRP_ITEMS, I + GRP + 2 * j + half)
                            pe.wait_ge(split_done, at(g, GRP_UNITS, unit + 3))
                            three_passes(s, parts(w_hi, unit, GRP, half * P), parts(w_lo, unit, GRP, half * P),
                                         hid_hi, hid_lo, None if j + half else hidden).then_inc(unit_done if half else mini_done, 1)
                        mods(GRP + j)

            out_proj(0)
            norm(1)
            mlp(0)
            norm(2)

            I0, U0 = AT_MIX[1].items, AT_MIX[1].units
            pe.wait_ge(h_ready, 4 * KT)
            with pe.Fori(0, KT) as b:
                project(b, BLK_ITEMS, I0, BLK_UNITS, U0).then_inc(unit_done, 1)
                project(b, BLK_ITEMS, I0 + 1, BLK_UNITS, U0 + 1).then_inc(unit_done, 1)
                for j in range(4):
                    s = take_set(b, BLK_ITEMS, I0 + 2 + j)
                    if j == 0:
                        pe.wait_ge(gate_landed, at(b, 64, 64))
                        pe.wait_ge(xc_ready, b + 2)
                    for c in range(BANKS):
                        last = pe.matmul(psum[:, s, c, 0:CH], gate_w[:, j, :], xc[:, c * CH:(c + 1) * CH], start=True, stop=True)
                    last.then_inc(mini_done, 1)
            out_proj(1)
            norm(3)
            mlp(1)
            norm(4)
            for n in range(NCH):
                s = take_set(None, 0, AT_END.items + n)
                if n == 0:
                    pe.wait_ge(y_ready, KT)
                for k in range(KT):
                    last = pe.transpose(psum[:, s, k // 4, k % 4 * P:(k % 4 + 1) * P], y_cols[:, k, n * P:(n + 1) * P], ident[:])
                last.then_inc(mini_done, 1)

        @block.scalar
        def _(act):
            steps = Steps()
            for dst, src in par_loads:
                act.dma_start(dst, src).then_inc(par_landed, 16)

            item_out(act, None, 0, 0)
            act.activation(cond[:].rearrange("p c k -> p (c k)"), par[:, R_C:R_C + 2 * KT], ACT.Silu).then_inc(cond_ready, 1)
            for n in range(NCH):
                s = (1 + n) % 2
                act.wait_ge(mini_done, 2 + n)
                act.activation(x[:, :, n * P:(n + 1) * P], psum[:, s, 0:2, :].rearrange("p b (k t) -> p (b k) t", k=4),
                               ACT.Copy).then_inc(read_out[s], 1)
            act.wait_ge(neg_abs_ready, 1)
            act.activation(sp_exp[:], sp_neg[:], ACT.Exp).then_inc(exp_ready, 1)
            act.wait_ge(decays_ready, 2)
            for n in range(HEADS):
                log_f, log_b = lg[:, n:n + 1], lg[:, HEADS + n:HEADS + n + 1]
                act.activation(exps[:, 0, n, :], consts[:, C_DF:C_DF + P], ACT.Exp, scale=log_f)
                act.activation(exps[:, 1, n, :], consts[:, C_DB:C_DB + P], ACT.Exp, scale=log_b)
                act.activation(q_dec[:, 0, n, :], consts[:, C_QF:C_QF + P], ACT.Exp, scale=log_f)
                act.activation(q_dec[:, 1, n, :], consts[:, C_QB:C_QB + P], ACT.Exp, scale=log_b)
                act.activation(k_dec[:, 0, n:n + 1], consts[:, C_KF:C_KF + 1], ACT.Exp, scale=log_f)
                act.activation(k_dec[:, 1, n:n + 1], consts[:, C_KB:C_KB + 1], ACT.Exp, scale=log_b)
            act.activation(g_chunk[:].rearrange("p d h -> p (d h)"), lg[:], ACT.Exp, scale=float(P)).then_inc(powers_ready, 1)

            def root_mean_square(n):
                for k in range(KT):
                    if n in (1, 3) or (n == 0 and k == 0):
                        item_out(act, None, 0, AT_NORM[n].items - (KT - k if n else 1))
                        if n == 0:
                            item_out(act, None, 0, AT_NORM[n].items - 2)
                    elif n:
                        item_out(act, None, 0, AT_NORM[n].items - (KT - k))
                    if k >= 3:
                        act.wait_ge(sq_added, n * (KT - 1) + k - 2)
                    dst = sumsq if k == 0 else square(n, k)
                    act.activation(dst[:], x[:, k, :], ACT.Square).then_inc(sq_ready, 1)
                s = AT_NORM[n].items % 2
                act.wait_ge(mini_done, AT_NORM[n].minis + 1)
                act.activation(by_bank(rstd[:]), whole(s), ACT.Sqrt, bias=eps[:], scale=1.0 / D_MODEL).then_inc(read_out[s], 1)

            def modulated_tiles(n):
                before = (0, 2, 3, 5)[n] * KT
                act.wait_ge(gain_ready, n + 1)
                for k in range(KT):
                    act.wait_ge(scaled_ready, n * KT + k + 1)
                    if k >= 2:
                        act.wait_ge(h_ready, before + k - 1)
                    t, m = scaled[k % 2], modulated[k % 2]
                    for c, (start, end) in enumerate(((0, LAT), (LAT, TOK))):
                        act.activation(m[:, start:end], t[:, start:end], ACT.Identity, scale=gain[:, k, c:c + 1],
                                       bias=mod[:, n // 2, (SH1, SH2)[n % 2] + k, c:c + 1]).then_inc(act_step, 1)
                        made = steps.done()
                    act.wait_ge(act_step, made)
                    act.activation(h_hi[:, k, :], m[:], ACT.Copy).then_inc(part_hi, 1)

            def split_mix(l):
                act.wait_ge(unit_done, AT_OUT[l].units)
                if l == 0:
                    item_out(act, None, 0, AT_OUT[0].items - 2)
                    act.wait_ge(gm_out, 1 + HEADS)
                else:
                    act.wait_ge(lru_done, 1 + KT)
                for k in range(KT):
                    act.activation(h_hi[:, k, :], mix[:, k, :], ACT.Copy).then_inc(part_hi, 1)

            def mlp(l):
                I, U = AT_MLP[l].items, AT_MLP[l].units
                with act.Fori(0, GROUPS) as g:
                    for j in range(GRP):
                        s = (I + j) % 2
                        chunks = BANKS * (l * GRP * GROUPS + j)
                        act.wait_ge(unit_done, at(g, GRP_UNITS, U + j + 1))
                        act.wait_ge(relu2_ready, at(g, BANKS * GRP, chunks + 1))
                        act.activation(by_bank(relu[:]), whole(s), ACT.Relu).then_inc(read_out[s], 1)
                        for c in range(BANKS):
                            act.wait_ge(relu2_ready, at(g, BANKS * GRP, chunks + c + 2))
                            act.activation(hid_hi[:, j, c * CH:(c + 1) * CH], relu2[:, c * CH:(c + 1) * CH],
                                           ACT.Copy).then_inc(hid_part_hi, 1)

            root_mean_square(0)
            modulated_tiles(0)

            I0, U0, M0 = AT_MIX[0].items, AT_MIX[0].units, AT_MIX[0].minis
            act.wait_ge(x_spilled, 16)
            with act.Fori(0, HEADS) as h:
                steps.enter(h, 9)

                def unit(n):
                    act.wait_ge(unit_done, at(h, HEAD_UNITS, U0 + n + 1))

                def mini(n):
                    act.wait_ge(mini_done, at(h, HEAD_MINIS, M0 + n + 1))

                def swap():
                    for q in range(4):
                        last = act.activation(swapped[32 * q:32 * q + 32, 0:LAT],
                                              turned[32 * (q ^ 1):32 * (q ^ 1) + 32, 0:LAT], ACT.Copy)
                    return last

                unit(0)
                act.activation(by_bank(turned[:]), whole(I0 % 2), ACT.Copy, scale=float(P) ** -0.5).then_inc(read_out[I0 % 2], 1)
                item_out(act, h, HEAD_ITEMS, I0)
                swap().then_inc(projected, 1)
                unit(1)
                s = (I0 + 1) % 2
                act.activation(by_bank(v_raw[:]), whole(s), ACT.Copy).then_inc(read_out[s], 1)
                unit(2)
                act.wait_ge(k_ready, h + 1)
                s = (I0 + 3) % 2
                act.activation(by_bank(turned[:]), whole(s), ACT.Copy).then_inc(read_out[s], 1)
                item_out(act, h, HEAD_ITEMS, I0 + 3)
                swap().then_inc(projected, 1)
                mini(1)
                s = (I0 + 4) % 2
                act.activation(by_bank(v_row[:]), whole(s), ACT.Copy).then_inc(read_out[s], 1)
                unit(3)
                s = (I0 + 5) % 2
                act.activation(by_bank(v_raw[:]), whole(s), ACT.Silu).then_inc(read_out[s], 1)
                unit(4)
                s = (I0 + 8) % 2
                act.activation(by_bank(kT[:]), whole(s), ACT.Gelu_apprx_tanh).then_inc(read_out[s], 1)
                mini(5)
                s = (I0 + 10) % 2
                act.activation(by_bank(qT[:]), whole(s), ACT.Copy).then_inc(read_out[s], 1)
                unit(5)
                s = (I0 + 11) % 2
                act.activation(by_bank(k_fwd[:]), whole(s), ACT.Gelu_apprx_tanh).then_inc(read_out[s], 1)
                act.wait_ge(o_var, h + 1)
                act.activation(row_rstd[:], mean_var[:, :, 1], ACT.Sqrt, bias=eps[:]).then_inc(o_root, 1)
                mini(7)
                s = (I0 + 13) % 2
                for n in range(NCH):
                    act.activation(chunk(turned, n), part(s, n), ACT.Square, accum_out=vf_sum[:, n:n + 1]).then_inc(act_step, 1)
                    summed = steps.done()
                act.activation(by_bank(kT[:]), whole(s), ACT.Copy).then_inc(read_out[s], 1)
                act.wait_ge(act_step, summed)
                act.activation(vf_rstd[:], vf_sum[:], ACT.Sqrt, bias=eps[:], scale=1.0 / P).then_inc(vf_root, 1)
                mini(8)
                s = (I0 + 14) % 2
                act.activation(by_bank(tile_of(mix, h)), whole(s), ACT.Copy).then_inc(read_out[s], 1)
            steps.leave(HEADS)
            split_mix(0)
            root_mean_square(1)
            modulated_tiles(1)
            mlp(0)
            root_mean_square(2)
            modulated_tiles(2)

            I0, U0, M0 = AT_MIX[1].items, AT_MIX[1].units, AT_MIX[1].minis
            with act.Fori(0, KT) as b:
                act.wait_ge(unit_done, at(b, BLK_UNITS, U0 + 1))
                act.wait_ge(xc_ready, b + 1)
                s = I0 % 2
                act.activation(xin[:, LPAD:LPAD + LATC * CH].rearrange("p (c t) -> p c t", c=LATC), psum[:, s, 0:LATC, 0:CH], ACT.Copy)
                act.activation(xin[:, LPAD + LATC * CH:LPAD + LAT], psum[:, s, LATC, 0:LREST], ACT.Copy)
                act.activation(xin[:, CTX0 + LPAD:CTX0 + LPAD + CTX], psum[:, s, LATC, LREST:CH], ACT.Copy).then_inc(read_out[s], 1)
                act.wait_ge(unit_done, at(b, BLK_UNITS, U0 + 2))
                act.wait_ge(lru_done, b + 1)
                s = (I0 + 1) % 2
                act.activation(by_bank(gelu_gate[:]), whole(s), ACT.Gelu_apprx_tanh).then_inc(read_out[s], 1)
                for j in range(4):
                    d, kind = j // 2, j % 2
                    s = (I0 + 2 + j) % 2
                    act.wait_ge(mini_done, at(b, BLK_MINIS, M0 + j + 1))
                    act.activation(by_bank((gated if kind else rate)[d][:]), whole(s), ACT.Sigmoid,
                                   bias=col(par, b + ((R_GX if kind else R_GA) + d * KT))).then_inc(read_out[s], 1)
                for d in range(2):
                    item_out(act, b, BLK_ITEMS, I0 + 2 + 2 * d)
                    act.activation(rate[d][:], rate[d][:], ACT.Tanh, scale=col(lru_rate, b + d * KT)).then_inc(tanh_ready, 1)
                for d in range(2):
                    act.wait_ge(tanh_ready, at(b, 2, d + 1))
                    act.activation(root[d][:], rate[d][:], ACT.Sqrt).then_inc(root_ready, 1)
            split_mix(1)
            root_mean_square(3)
            modulated_tiles(3)
            mlp(1)
            root_mean_square(4)
            for n in range(NCH):
                s = (AT_END.items + n) % 2
                act.wait_ge(mini_done, AT_END.minis + n + 1)
                act.activation(y_rows[:, n, :].rearrange("p (k t) -> p k t", k=KT),
                               psum[:, s, 0:2, :].rearrange("p b (k t) -> p (b k) t", k=4), ACT.Copy).then_inc(read_out[s], 1)

        @block.vector
        def _(dve):
            steps = Steps()

            def after(value):
                dve.wait_ge(dve_step, value)

            dve.nop().then_inc(relu2_ready, 1)
            dve.nop().then_inc(hid_ready, 1)
            dve.nop().then_inc(gm_out, 1)
            dve.nop().then_inc(lru_done, 1)
            dve.wait_ge(mini_done, 1)
            dve.tensor_copy(par[:], psum[:, 0, 0, 0:2 * P])
            dve.tensor_copy(wsT[:].rearrange("p (b g) t -> p b (g t)", b=2), psum[:, 0, 1:3, 0:2 * P])
            dve.tensor_copy(bs_all[:].rearrange("p (b g) t -> p b (g t)", b=2), psum[:, 0, 1:3, 2 * P:4 * P])
            dve.tensor_copy(sp_z[:, 2 * HEADS:24], psum[:, 0, 0, R_LAM:R_LAM + 2 * KT])
            dve.tensor_copy(sp_z[:, 0:2 * HEADS], psum[:, 0, 0, 2 * P:2 * P + 2 * HEADS]).then_inc(read_out[0], 1)
            dve.tensor_copy(ident[:], consts[:, C_ID:C_ID + P])
            item_out(dve, None, 0, 0)
            dve.tensor_scalar(sp_neg[:], sp_z[:], -1.0, None, ALU.mult).then_inc(dve_step, 1)
            after(steps.done())
            dve.tensor_scalar(sp_max[:], sp_neg[:], 0.0, None, ALU.max).then_inc(dve_step, 1)
            after(steps.done())
            dve.tensor_tensor(sp_neg[:], sp_neg[:], sp_z[:], ALU.min).then_inc(neg_abs_ready, 1)
            dve.wait_ge(exp_ready, 1)
            dve.tensor_scalar(sp_r[:], sp_exp[:], 2.0, None, ALU.add).then_inc(dve_step, 1)
            after(steps.done())
            dve.reciprocal(sp_r[:], sp_r[:]).then_inc(dve_step, 1)
            after(steps.done())
            dve.tensor_tensor(sp_r[:], sp_exp[:], sp_r[:], ALU.mult).then_inc(dve_step, 1)
            after(steps.done())
            dve.tensor_tensor(sp_r2[:], sp_r[:], sp_r[:], ALU.mult).then_inc(dve_step, 1)
            after(steps.done())
            dve.tensor_scalar(sp_q[:], sp_r2[:], 1.0 / 15, None, ALU.mult).then_inc(dve_step, 1)
            after(steps.done())
            for odd in (13, 11, 9, 7, 5, 3):
                dve.scalar_tensor_tensor(out=sp_q[:], in0=sp_q[:], scalar=1.0 / odd, in1=sp_r2[:],
                                         op0=ALU.add, op1=ALU.mult).then_inc(dve_step, 1)
                after(steps.done())
            dve.scalar_tensor_tensor(out=sp_q[:], in0=sp_q[:], scalar=1.0, in1=sp_r[:], op0=ALU.add, op1=ALU.mult).then_inc(dve_step, 1)
            after(steps.done())
            dve.scalar_tensor_tensor(out=sp_q[:], in0=sp_q[:], scalar=2.0, in1=sp_max[:], op0=ALU.mult, op1=ALU.add).then_inc(dve_step, 1)
            after(steps.done())
            dve.tensor_scalar(lg[:], sp_q[:, 0:2 * HEADS], -1.0, None, ALU.mult).then_inc(decays_ready, 1)
            dve.tensor_scalar(lru_rate[:], sp_q[:, 2 * HEADS:24], LRU_C / 2, None, ALU.mult).then_inc(decays_ready, 1)
            dve.wait_ge(powers_ready, 1)
            for d, m in enumerate((C_MF, C_MB)):
                dve.tensor_tensor(exps[:, d], exps[:, d], consts[:, m:m + P].unsqueeze(1).to_broadcast([P, HEADS, P]),
                                  ALU.mult).then_inc(dve_step, 1)
                masked = steps.done()
            after(masked)
            dve.tensor_tensor(mask[:], exps[:, 0], exps[:, 1], ALU.add).then_inc(dve_step, 1)
            steps.done()

            def mods_out(l, first, count, used):
                dve.wait_ge(mod_used, used)
                if isinstance(first, int):
                    dst, src = mod[:, l, first:first + count, :], mod_psum[:, (l * MODS + first) * 2:(l * MODS + first + count) * 2]
                    bias = par[:, R_MODB + l * MODS + first:R_MODB + l * MODS + first + count]
                else:
                    dst, src = mod[:, l, ds(first, count), :], mod_psum[:, ds(first * 2 + 2 * l * MODS, 2 * count)]
                    bias = par[:, ds(first + (R_MODB + l * MODS), count)]
                dve.tensor_tensor(dst, src.rearrange("p (m c) -> p m c", c=2), bias.unsqueeze(2).to_broadcast([P, count, 2]),
                                  ALU.add).then_inc(mod_read, 1)

            def gains(n, batches):
                l, scale, row = n // 2, (SC1, SC2)[n % 2], (R_NMIX, R_NMLP)[n % 2]
                dve.wait_ge(mod_read, batches)
                dve.scalar_tensor_tensor(out=gain[:], in0=mod[:, l, scale:scale + KT, :], scalar=1.0,
                                         in1=par[:, row + l * KT:row + (l + 1) * KT].unsqueeze(2).to_broadcast([P, KT, 2]),
                                         op0=ALU.add, op1=ALU.mult).then_inc(gain_ready, 1)

            def root_mean_square(n):
                for k in range(1, KT):
                    dve.wait_ge(sq_ready, n * KT + k + 1)
                    if k > 1:
                        dve.wait_ge(sq_added, n * (KT - 1) + k - 1)
                    dve.tensor_tensor(sumsq[:], sumsq[:], square(n, k)[:], ALU.add).then_inc(sq_added, 1)
                item_out(dve, None, 0, AT_NORM[n].items)
                dve.reciprocal(rstd[:], rstd[:]).then_inc(dve_step, 1)
                after(steps.done())

            def low_part(k, of, value):
                dve.wait_ge(part_hi, value)
                dve.tensor_tensor(h_lo[:, k, :], of, h_hi[:, k, :].bitcast(F32), ALU.subtract).then_inc(h_ready, 1)

            def modulated_tiles(n):
                before = (0, 2, 3, 5)[n] * KT
                for k in range(KT + 1):
                    if k < KT:
                        if k >= 2:
                            dve.wait_ge(part_hi, before + k - 1)
                        dve.tensor_tensor(scaled[k % 2][:], x[:, k, :], rstd[:], ALU.mult).then_inc(scaled_ready, 1)
                    if k:
                        low_part(k - 1, modulated[(k - 1) % 2][:], before + k)

            def split_mix(l):
                for k in range(KT):
                    low_part(k, mix[:, k, :], (3 * l + 1) * KT + k + 1)

            def update(s, k, l, gate):
                for src, dst, c in pieces(s, x[:, k, :]):
                    last = dve.scalar_tensor_tensor(out=dst, in0=src, scalar=mod[:, l, gate + k, c:c + 1], in1=dst,
                                                    op0=ALU.mult, op1=ALU.add)
                return last

            def out_proj(l):
                dve.wait_ge(x_back, 16 * (l + 1))
                for k in range(KT):
                    s = (AT_OUT[l].items + k) % 2
                    dve.wait_ge(unit_done, AT_OUT[l].units + k + 1)
                    update(s, k, l, G1).then_inc(read_out[s], 1)

            def mlp(l):
                I, U, M = AT_MLP[l].items, AT_MLP[l].units, AT_MLP[l].minis
                with dve.Fori(0, GROUPS) as g:
                    for j in range(GRP):
                        chunks = BANKS * (l * GRP * GROUPS + j)
                        item_out(dve, g, GRP_ITEMS, I + j)
                        dve.wait_ge(hid_ready, at(g, BANKS * GRP, chunks + 1))
                        for c in range(BANKS):
                            t = relu[:, c * CH:(c + 1) * CH]
                            dve.tensor_tensor(relu2[:, c * CH:(c + 1) * CH], t, t, ALU.mult).then_inc(relu2_ready, 1)
                        for c in range(BANKS):
                            dve.wait_ge(hid_part_hi, at(g, BANKS * GRP, chunks + c + 1))
                            t = slice(c * CH, (c + 1) * CH)
                            dve.tensor_tensor(hid_lo[:, j, t], relu2[:, t], hid_hi[:, j, t].bitcast(F32),
                                              ALU.subtract).then_inc(hid_ready, 1)
                    for k in range(2 * GRP):
                        s = (I + GRP + k) % 2
                        if k % 2 == 0:
                            dve.wait_ge(mini_done, at(g, GRP_MINIS, M + k // 2 + 1))
                        else:
                            dve.wait_ge(unit_done, at(g, GRP_UNITS, U + GRP + k // 2 + 1))
                        update(s, k, l, G2).then_inc(read_out[s], 1)
                    if l == 0:
                        mods_out(1, g * GRP_MODS, GRP_MODS, at(g, GRP_MODS, 2 + MODS + GRP_MODS))

            mods_out(0, 0, FIRST_MODS, 2 + FIRST_MODS)
            gains(0, 1)
            root_mean_square(0)
            modulated_tiles(0)

            I0, M0 = AT_MIX[0].items, AT_MIX[0].minis
            dve.wait_ge(x_spilled, 16)
            with dve.Fori(0, HEADS) as h:
                steps.enter(h, 32)

                def mini(n):
                    dve.wait_ge(mini_done, at(h, HEAD_MINIS, M0 + n + 1))

                def rotate(dst, ready):
                    dve.tensor_tensor(dst[:, 0:LAT], turned[:, 0:LAT], rope[:, 0, :], ALU.mult).then_inc(dve_step, 1)
                    steps.done()
                    dve.tensor_tensor(swapped[:, 0:LAT], swapped[:, 0:LAT], rope[:, 1, :], ALU.mult).then_inc(dve_step, 1)
                    after(steps.done())
                    dve.tensor_tensor(dst[:, 0:LAT], dst[:, 0:LAT], swapped[:, 0:LAT], ALU.add).then_inc(dve_step, 1)
                    steps.done()
                    return dve.tensor_copy(dst[:, LAT:TOK], turned[:, LAT:TOK])

                def by_chunk(t):
                    return t.rearrange("p (n t) -> p n t", t=P)

                dve.wait_ge(projected, h * 2 + 1)
                rotate(kT, k_ready).then_inc(k_ready, 1)
                mini(0)
                s = (I0 + 2) % 2
                dve.wait_ge(state_out, h * 32 + 32)
                dve.wait_ge(gm_out, h + 1)
                dve.tensor_scalar(by_bank(k_fwd[:]), whole(s), col(k_dec[:, 0, :], h), None, ALU.mult)
                dve.tensor_scalar(by_bank(k_bwd[:]), whole(s), col(k_dec[:, 1, :], h), None, ALU.mult).then_inc(read_out[s], 1)
                dve.wait_ge(projected, h * 2 + 2)
                rotate(qT, q_ready).then_inc(dve_step, 1)
                after(steps.done())
                for d, t in enumerate((turned, swapped)):
                    last = dve.tensor_tensor(by_chunk(t[:, 0:LAT]), by_chunk(qT[:, 0:LAT]),
                                             tile_of(q_dec[:, d], h).unsqueeze(1).to_broadcast([P, LCH, P]), ALU.mult)
                last.then_inc(q_ready, 1)
                mini(2)
                dve.wait_ge(state_in, h * 32 + 32)
                s = (I0 + 6) % 2
                dve.tensor_copy(chunk(s_bwd, LCH), part(s, LCH)).then_inc(dve_step, 1)
                steps.done()
                for n in range(LCH - 1, 0, -1):
                    last = dve.scalar_tensor_tensor(out=chunk(s_bwd, n - 1), in0=chunk(s_bwd, n), scalar=col(g_chunk[:, 1, :], h),
                                                    in1=part(s, n), op0=ALU.mult, op1=ALU.add)
                    if n > 1:
                        last.then_inc(dve_step, 1)
                        after(steps.done())
                last.then_inc(read_out[s], 1)
                mini(3)
                s = (I0 + 7) % 2
                dve.tensor_tensor(probs[:].rearrange("p (c n t) -> p c n t", c=BANKS, t=P),
                                  whole(s).rearrange("p c (n t) -> p c n t", t=P),
                                  tile_of(mask, h).unsqueeze(1).unsqueeze(1).to_broadcast([P, BANKS, BANKS, P]),
                                  ALU.mult).then_inc(read_out[s], 1)
                mini(4)
                s = (I0 + 9) % 2
                dve.tensor_copy(chunk(k_bwd, LCH), part(s, LCH)).then_inc(dve_step, 1)
                steps.done()
                for n in range(LCH - 1):
                    last = dve.scalar_tensor_tensor(out=chunk(k_bwd, n + 1), in0=s0_fwd[:] if n == 0 else chunk(k_bwd, n),
                                                    scalar=col(g_chunk[:, 0, :], h), in1=part(s, n), op0=ALU.mult, op1=ALU.add)
                    if n < LCH - 2:
                        last.then_inc(dve_step, 1)
                        after(steps.done())
                last.then_inc(read_out[s], 1)
                mods_out(0, h * HEAD_MODS + FIRST_MODS, HEAD_MODS, at(h, HEAD_MODS, 2 + FIRST_MODS + HEAD_MODS))
                mini(6)
                s = (I0 + 12) % 2
                for n in range(NCH):
                    dve.bn_stats(stats[:, n, :], part(s, n)).then_inc(dve_step, 1)
                    done = steps.done()
                after(done)
                dve.sem_inc(passed, 1)
                for n in range(NCH):
                    last = dve.bn_aggr(mean_var[:, n, :], stats[:, n, :])
                last.then_inc(o_var, 1)
                dve.wait_ge(o_var, h + 1)
                dve.wait_ge(o_root, h + 1)
                dve.reciprocal(row_rstd[:], row_rstd[:]).then_inc(dve_step, 1)
                after(steps.done())
                for n in range(NCH):
                    last = dve.tensor_scalar(chunk(v_raw, n), part(s, n), mean_var[:, n, 0:1], row_rstd[:, n:n + 1],
                                             ALU.subtract, ALU.mult)
                last.then_inc(read_out[s], 1)
                item_out(dve, h, HEAD_ITEMS, I0 + 12)
                dve.tensor_tensor(v_raw[:], v_raw[:], qT[:], ALU.mult).then_inc(o_ready, 1)
                dve.wait_ge(vf_root, h + 1)
                dve.reciprocal(vf_rstd[:], vf_rstd[:]).then_inc(dve_step, 1)
                after(steps.done())
                dve.tensor_tensor(by_chunk(kT[:]), by_chunk(kT[:]), vf_rstd[:].unsqueeze(2).to_broadcast([P, NCH, P]),
                                  ALU.mult).then_inc(vf_ready, 1)
                mini(9)
                s = (I0 + 15) % 2
                dve.tensor_tensor(probs[:].rearrange("p (c n t) -> p c n t", c=BANKS, t=P),
                                  whole(s).rearrange("p c (n t) -> p c n t", t=P),
                                  tile_of(bs_all, h).unsqueeze(1).unsqueeze(1).to_broadcast([P, BANKS, BANKS, P]),
                                  ALU.add).then_inc(read_out[s], 1)
                item_out(dve, h, HEAD_ITEMS, I0 + 15)
                dve.tensor_tensor(tile_of(mix, h + HEADS), probs[:], k_fwd[:], ALU.mult).then_inc(gm_out, 1)
            steps.leave(HEADS)
            split_mix(0)
            out_proj(0)
            gains(1, 1 + HEADS)
            root_mean_square(1)
            modulated_tiles(1)
            mlp(0)
            gains(2, 1 + HEADS + GROUPS)
            root_mean_square(2)
            modulated_tiles(2)

            I0 = AT_MIX[1].items
            dve.memset(xin[:, 0:LPAD], 0.0)
            dve.memset(xin[:, LPAD + LAT:CTX0 + LPAD], 0.0)
            dve.memset(xin[:, CTX0 + LPAD + CTX:], 0.0).then_inc(xc_ready, 1)
            dve.wait_ge(x_spilled, 32)
            runs = ((0, LAT, 0), (LAT, TOK, CTX0))
            with dve.Fori(0, KT) as b:
                steps.enter(b, 24)
                item_out(dve, b, BLK_ITEMS, I0)
                for j in range(4):
                    for start, end, row in runs:
                        src, w = xin[:, row + j:row + j + end - start], col(par, b + (R_CONVW + j * KT))
                        if j == 0:
                            last = dve.tensor_scalar(xc[:, start:end], src, w, col(par, b + R_CONVB), ALU.mult, ALU.add)
                        else:
                            last = dve.scalar_tensor_tensor(out=xc[:, start:end], in0=src, scalar=w, in1=xc[:, start:end],
                                                            op0=ALU.mult, op1=ALU.add)
                        if j < 3:
                            last.then_inc(dve_step, 1)
                            done = steps.done()
                    if j < 3:
                        after(done)
                last.then_inc(xc_ready, 1)
                for d in range(2):
                    dve.wait_ge(tanh_ready, at(b, 2, d + 1))
                    dve.tensor_scalar(denom[d][:], rate[d][:], 1.0, None, ALU.add).then_inc(dve_step, 1)
                    added = steps.done()
                    item_out(dve, b, BLK_ITEMS, I0 + 3 + 2 * d)
                    dve.wait_ge(xc_ready, b + 2)
                    dve.tensor_tensor(gated[d][:], gated[d][:], xc[:], ALU.mult).then_inc(dve_step, 1)
                    steps.done()
                    after(added)
                    dve.reciprocal(denom[d][:], denom[d][:]).then_inc(dve_step, 1)
                    after(steps.done())
                    dve.wait_ge(root_ready, at(b, 2, d + 1))
                    dve.tensor_tensor(root[d][:], root[d][:], denom[d][:], ALU.mult).then_inc(dve_step, 1)
                    rooted = steps.done()
                    dve.tensor_scalar(rate[d][:], denom[d][:], 2.0, 1.0, ALU.mult, ALU.subtract).then_inc(dve_step, 1)
                    steps.done()
                    after(rooted)
                    dve.scalar_tensor_tensor(out=gated[d][:], in0=root[d][:], scalar=2.0, in1=gated[d][:],
                                             op0=ALU.mult, op1=ALU.mult).then_inc(dve_step, 1)
                    after(steps.done())
                    for start, end, _row in runs:
                        step = 1 if d == 0 else -1
                        view = lambda t: t[:, start:end][:, ::step]
                        first = col(par, b + (R_LF, R_LB)[d]) if start == 0 else 0.0
                        dve.tensor_tensor_scan(view(denom[d]), view(rate[d]), view(gated[d]), first,
                                               ALU.mult, ALU.add).then_inc(dve_step, 1)
                        scanned = steps.done()
                after(scanned)
                dve.tensor_copy(col(lru_last[:, 0, :], b), denom[0][:, TOK - 1:TOK])
                dve.tensor_copy(col(lru_last[:, 1, :], b), denom[1][:, LAT:LAT + 1]).then_inc(dve_step, 1)
                after(steps.done())
                dve.tensor_tensor(denom[1][:], denom[1][:], denom[0][:], ALU.add).then_inc(dve_step, 1)
                after(steps.done())
                item_out(dve, b, BLK_ITEMS, I0 + 1)
                dve.tensor_tensor(tile_of(mix, b), denom[1][:], gelu_gate[:], ALU.mult).then_inc(lru_done, 1)
            steps.leave(KT)
            split_mix(1)
            out_proj(1)
            gains(3, 1 + HEADS + GROUPS)
            root_mean_square(3)
            modulated_tiles(3)
            mlp(1)
            root_mean_square(4)
            for k in range(KT):
                dve.scalar_tensor_tensor(out=y_cols[:, k, :], in0=x[:, k, :], scalar=par[:, R_FN + k:R_FN + k + 1], in1=rstd[:],
                                         op0=ALU.mult, op1=ALU.mult).then_inc(y_ready, 1)


def constants():
    i = np.arange(P, dtype=np.float64)
    ahead = i[None, :] - i[:, None]
    table = np.zeros((P, C_ALL), np.float32)
    for at, block in ((C_ID, np.eye(P)), (C_DF, np.maximum(ahead, 0)), (C_DB, np.maximum(-ahead - 1, 0)),
                      (C_MF, ahead >= 0), (C_MB, ahead < 0),
                      (C_QF, np.broadcast_to(i + 1, (P, P))), (C_QB, np.broadcast_to(P - 1 - i, (P, P)))):
        table[:, at:at + P] = block
    table[:, C_KF], table[:, C_KB] = P - 1 - i, i
    pos = np.arange(LAT)
    half = P // 2
    freq = (np.float32(ROPE_BASE) ** (-np.arange(half // 2, dtype=np.float32) / np.float32(half // 2))).astype(np.float32)
    turns = np.zeros((P, 2, LAT), np.float32)
    for part, p in enumerate((pos // GRID_W, pos % GRID_W)):
        angle = (p.astype(np.float32)[None, :] * freq[:, None]).astype(np.float64)
        for side, sign in enumerate((-1.0, 1.0)):
            rows = slice(part * half + side * half // 2, part * half + (side + 1) * half // 2)
            turns[rows, 0], turns[rows, 1] = np.cos(angle), sign * np.sin(angle)
    return table, turns


_INS = ['x_prompt', 'x_sample', 'c', 'c_ctx', 'state_ret_fwd', 'state_ret_bwd', 'state_lru_fwd', 'state_lru_bwd',
        'mod_w', 'mod_b', 'norm_mix', 'norm_mlp', 'mlp_w1', 'mlp_w2', 'ab_w_in', 'ab_w_out', 'ret_decay_fwd',
        'ret_decay_bwd', 'gmlp_ws', 'gmlp_bs', 'lru_w_in', 'lru_conv_w', 'lru_conv_b', 'lru_gate_a_w', 'lru_gate_a_b',
        'lru_gate_x_w', 'lru_gate_x_b', 'lru_lambda', 'lru_w_out', 'final_norm']
_OUTS = [('y_prompt', (1, CTX, D_MODEL)), ('y_sample', (1, LAT, D_MODEL)), ('new_ret_fwd', (1, 1, HEADS, P, P)),
         ('new_ret_bwd', (1, 1, HEADS, P, P)), ('new_lru_fwd', (1, 1, D_MODEL)), ('new_lru_bwd', (1, 1, D_MODEL))]


def kernel(**inputs):
    import concourse.bacc as bacc
    from concourse.bass_utils import run_bass_kernel_spmd as run

    nc = bacc.Bacc("TRN2", target_bir_lowering=False, num_devices=1)
    arrays, args = {}, {}
    named = {name: np.ascontiguousarray(inputs[name]) for name in _INS}
    named['consts'], named['rope'] = constants()
    for name, value in named.items():
        arrays[f"in_{name}"] = value
        args[name] = nc.dram_tensor(f"in_{name}", value.shape, F32, kind="ExternalInput").ap()
    for name, shape in _OUTS:
        args[name] = nc.dram_tensor(f"out_{name}", shape, F32, kind="ExternalOutput").ap()
    with nc.allow_non_contiguous_dma(reason="final states of the RG-LRU lie by columns"):
        build(nc, args)
    r = run(nc, [arrays], core_ids=[0])
    return tuple(r.results[0][f"out_{name}"] for name, _ in _OUTS)
```

```python
from contextlib import ExitStack

import numpy as np

import concourse.bass as bass
from concourse import mybir

F32 = mybir.dt.float32
F32R = mybir.dt.float32r
ALU = mybir.AluOpType
ACT = mybir.ActivationFunctionType
ds = bass.ds

P = 128
D_MODEL = 1024
LAT = 1024
CTX = 128
TOK = LAT + CTX
BANKS = 3
CH = TOK // BANKS
NCH = TOK // P
LCH = LAT // P
KT = D_MODEL // P
D_FF = 4 * D_MODEL
HEADS = 4
HD = HEADS * P
LRU_C = 8.0
EPS = 1e-6
GRID_W = 64
ROPE_BASE = 10000.0
GRP = 4
GROUPS = D_FF // P // GRP
MODS = 6 * KT
SH1, SC1, G1, SH2, SC2, G2 = (n * KT for n in range(6))

SECTIONS = (1, 2, 0, 3, 5, 4)

R_MODB, R_NMIX, R_NMLP = 0, 96, 112
R_CONVW, R_CONVB, R_GA, R_GX, R_LAM, R_LF, R_LB, R_FN, R_C = (
    128 + n for n in (0, 32, 40, 56, 72, 88, 96, 104, 112))

C_ID, C_DF, C_DB, C_MF, C_MB, C_QF, C_QB, C_KF, C_KB = 0, 128, 256, 384, 512, 640, 768, 896, 897
C_ALL = 898

HEAD_UNITS, HEAD_ITEMS, HEAD_MINIS, HEAD_MODS = 6, 16, 10, 8
COLS = TOK + 2
BLK_UNITS, BLK_ITEMS, BLK_MINIS = 2, 6, 4
GRP_UNITS, GRP_ITEMS, GRP_MINIS, GRP_MODS = 8, 12, 4, 6

START_ITEMS = NCH + 3
SCALE_ITEM, SHIFT_ITEM = START_ITEMS - 2, START_ITEMS - 1
FIRST_MODS = 2 * KT
FIRST_BATCHES = 2


class Place:

    def __init__(self, units, items, minis):
        self.units, self.items, self.minis = units, items, minis

    def after(self, units, items, minis):
        return Place(self.units + units, self.items + items, self.minis + minis)


AT_MIX = [Place(0, START_ITEMS, START_ITEMS), None]
AT_OUT = [AT_MIX[0].after(HEADS * HEAD_UNITS, HEADS * HEAD_ITEMS, HEADS * HEAD_MINIS), None]
AT_MLP = [AT_OUT[0].after(KT, KT, 0), None]
AT_MIX[1] = AT_MLP[0].after(GROUPS * GRP_UNITS, GROUPS * GRP_ITEMS, GROUPS * GRP_MINIS)
AT_OUT[1] = AT_MIX[1].after(KT * BLK_UNITS, KT * BLK_ITEMS, KT * BLK_MINIS)
AT_MLP[1] = AT_OUT[1].after(KT, KT, 0)
AT_END = AT_MLP[1].after(GROUPS * GRP_UNITS, GROUPS * GRP_ITEMS, GROUPS * GRP_MINIS)
UNITS = AT_END.units
H_NORM = (0, 2 * KT, 3 * KT, 5 * KT)
H_MIX = (KT, 4 * KT)
MIX_ORDER = ((0, 1, 2, 4, 5, 6, 3, 7), tuple(range(KT)))
LATE = (2, 1)
DVE_LOW = 2


class Steps:

    def __init__(self):
        self.base, self.n, self.loop, self.per = 0, 0, None, 0

    def enter(self, loop, per):
        self.base, self.n, self.loop, self.per = self.base + self.n, 0, loop, per

    def leave(self, times):
        assert self.n == self.per, f"a loop's iteration has {self.n} steps, not {self.per}"
        self.base, self.n, self.loop = self.base + times * self.per, 0, None

    def done(self):
        self.n += 1
        return self.base + self.n if self.loop is None else self.loop * self.per + (self.base + self.n)


def build(nc, a):
    with ExitStack() as ctx:
        here = [(nc.sbuf_base + 31) // 32 * 32]

        def region(size):
            at = here[0]
            here[0] += (size + 31) // 32 * 32
            assert here[0] <= nc.sbuf_usable_end, f"{here[0]} of {nc.sbuf_usable_end} bytes"
            return at

        def sb(name, shape, at=None, dtype=F32):
            size = 4 * int(np.prod(shape))
            return nc.alloc_sbuf_tensor_at(name, [P] + list(shape), dtype, offset=region(size) if at is None else at)

        TB = 4 * TOK
        x_at = region(KT * TB)
        x = sb("x", [KT, TOK], x_at)
        mix = sb("mix", [KT, TOK], x_at)
        h_at = region(2 * 4 * KT * COLS)
        h_hi = sb("h_hi", [KT, COLS], h_at, F32R)
        h_lo = sb("h_lo", [KT, COLS], h_at + 4 * KT * COLS, F32R)
        x_rows = sb("x_rows", [NCH, D_MODEL], h_at)
        scale_raw = sb("scale_raw", [KT, KT * P], h_at + 4 * NCH * D_MODEL)
        y_cols = sb("y_cols", [KT, TOK], h_at)
        y_rows = sb("y_rows", [NCH, D_MODEL], h_at + KT * TB)
        w_raw_at = region(4 * 2 * D_MODEL)
        w_raw = sb("w_raw", [2, D_MODEL], w_raw_at)
        w_hi = sb("w_hi", [2, D_MODEL], None, F32R)
        w_lo_at = region(4 * 2 * D_MODEL)
        w_lo = sb("w_lo", [2, D_MODEL], w_lo_at, F32R)
        mod_raw_at = region(4 * KT * P)
        mod_raw = sb("mod_raw", [2, KT // 2, P], mod_raw_at)
        mod_sum = sb("mod_sum", [2, 2, P])
        t_at = [region(TB) for _ in range(10)]
        tables_at = region(4 * 2 * LAT)

        def tile_at(n, name, dtype=F32):
            return sb(name, [TOK], t_at[n], dtype)

        turned = tile_at(0, "turned")
        swapped = tile_at(1, "swapped")
        kT = tile_at(2, "kT")
        v_raw = tile_at(3, "v_raw")
        k_fwd = tile_at(4, "k_fwd")
        k_bwd = tile_at(5, "k_bwd")
        qT = tile_at(6, "qT")
        v_row = tile_at(7, "v_row")
        probs = tile_at(8, "probs")
        s_bwd = tile_at(9, "s_bwd")
        rope = sb("rope", [2, LAT], tables_at)
        shift_raw = [sb(f"shift_raw_{k}", [KT * P], at) for k, at in enumerate(
            (t_at[8], t_at[9], mod_raw_at, w_raw_at + 4 * D_MODEL, w_lo_at + 4 * D_MODEL, t_at[0], t_at[1], t_at[4]))]
        mod_rows = sb("mod_rows", [2, KT * P], tables_at)
        sumsq = sb("sumsq", [TOK])
        rstd = sumsq
        square_start = [sb(f"square_start_{n}", [TOK], t_at[m]) for n, m in enumerate((3, 7))]
        square_out = sb("square_out", [TOK], tables_at)
        square_mlp = tile_at(8, "square_mlp")
        gained_start = [sb(f"gained_start_{n}", [COLS], t_at[m]) for n, m in enumerate((3, 7))]
        gained_out = [sb(f"gained_out_{k}", [COLS], t_at[0] + k * 4640) for k in range(KT)]
        gained_mlp = sb("gained_mlp", [COLS], tables_at)
        hid_hi = sb("hid_hi", [GRP, TOK], t_at[0], F32R)
        hid_lo = sb("hid_lo", [GRP, TOK], t_at[4], F32R)
        relu = sb("relu", [TOK], tables_at)
        relu2 = tile_at(9, "relu2")
        xc = tile_at(0, "xc")
        rate = [tile_at(1, "rate_f"), tile_at(3, "rate_b")]
        gated = [tile_at(2, "gated_f"), tile_at(4, "gated_b")]
        gelu_gate = tile_at(5, "gelu_gate")
        gate_raw = tile_at(8, "gate_raw")
        work = [tile_at(6, "work_f"), tile_at(7, "work_b")]
        LPAD, RPAD = 2, 1
        CTX0 = LPAD + LAT + RPAD
        xin = sb("xin", [CTX0 + LPAD + CTX + RPAD], tables_at)
        gate_w = sb("gate_w", [4, P], tables_at + 4 * 1160)
        par_rows = sb("par_rows", [2, P], t_at[0])
        ws_rows = sb("ws_rows", [HEADS, P], t_at[1])
        consts = sb("consts", [C_ALL], t_at[2])
        dec_row = sb("dec_row", [2 * HEADS], t_at[3])
        bs_row = sb("bs_row", [HEADS * P], t_at[4])
        exps = sb("exps", [2, HEADS, P], t_at[5])
        sp_z, sp_neg, sp_max, sp_exp, sp_r, sp_r2, sp_q = (
            sb(name, [24], t_at[6] + 128 * n) for n, name in enumerate(
                ("sp_z", "sp_neg", "sp_max", "sp_exp", "sp_r", "sp_r2", "sp_q")))
        ident = sb("ident", [P])
        ones = sb("ones", [P])
        mask = sb("mask", [HEADS, P])
        q_rows = sb("q_rows", [2, P])
        q_dec = sb("q_dec", [2, P])
        bs_all = sb("bs_all", [HEADS, P])
        wsT = sb("wsT", [HEADS, P])
        par = sb("par", [2 * P])
        cond = sb("cond", [2, KT])
        mod = sb("mod", [2, MODS, 2])
        gain = sb("gain", [KT, 2])
        k_dec = sb("k_dec", [2, HEADS])
        g_chunk = sb("g_chunk", [2, HEADS])
        lg = sb("lg", [2 * HEADS])
        lru_rate = sb("lru_rate", [2 * KT])
        lru_fall = sb("lru_fall", [2 * KT])
        eps = sb("eps", [1])
        s0_fwd = sb("s0_fwd", [P], t_at[1] + 4 * LAT)
        bias = sb("bias", [8, 2])
        stats = sb("stats", [NCH, 6])
        mean_var = sb("mean_var", [NCH, 2])
        row_rstd = sb("row_rstd", [NCH])
        vf_sum = sb("vf_sum", [NCH])
        vf_rstd = sb("vf_rstd", [NCH])
        lru_last = sb("lru_last", [2, KT])
        y_rstd = sb("y_rstd", [NCH])

        psum = ctx.enter_context(nc.psum_tensor("psum", [P, 2, BANKS, 512], F32))
        mod_psum = ctx.enter_context(nc.psum_tensor("mod_psum", [P, 512], F32))
        ssq_psum = ctx.enter_context(nc.psum_tensor("ssq_psum", [P, 512], F32))
        x_spill = nc.dram_tensor("x_spill", (P, KT * TOK), F32, kind="Internal").ap()

        def sem(name):
            return ctx.enter_context(nc.semaphore(name))

        raw_landed = [sem("raw_landed_0"), sem("raw_landed_1")]
        hi_done = sem("hi_done")
        split_done = sem("split_done")
        unit_done = sem("unit_done")
        mini_done = sem("mini_done")
        read_out = [sem("read_out_0"), sem("read_out_1")]
        mod_landed = [sem("mod_landed_0"), sem("mod_landed_1")]
        scale_landed = [sem(f"scale_landed_{k}") for k in range(KT)]
        shift_landed = [sem(f"shift_landed_{k}") for k in range(KT)]
        shift_ready = sem("shift_ready")
        mod_summed = sem("mod_summed")
        mod_used = sem("mod_used")
        mod_read = sem("mod_read")
        par_landed = [sem("par_landed_act"), sem("par_landed_sp")]
        rope_landed = sem("rope_landed")
        x_landed = [sem(f"x_landed_{n}") for n in range(NCH)]
        ones_set = sem("ones_set")
        cond_ready = sem("cond_ready")
        neg_abs_ready = sem("neg_abs_ready")
        exp_ready = sem("exp_ready")
        decays_ready = sem("decays_ready")
        powers_ready = sem("powers_ready")
        gain_ready = sem("gain_ready")
        sq_ready = sem("sq_ready")
        sq_added = sem("sq_added")
        gained_ready = sem("gained_ready")
        ssq_done = sem("ssq_done")
        ssq_read = sem("ssq_read")
        rstd_ready = sem("rstd_ready")
        scaled = sem("scaled")
        relu_ready = sem("relu_ready")
        activated = sem("activated")
        part_hi = sem("part_hi")
        h_ready = sem("h_ready")
        x_spilled = sem("x_spilled")
        x_back = [sem("x_back_first"), sem("x_back_rest")]
        projected = sem("projected")
        k_ready = sem("k_ready")
        q_ready = sem("q_ready")
        o_var = sem("o_var")
        o_root = sem("o_root")
        o_ready = sem("o_ready")
        vf_root = sem("vf_root")
        vf_ready = sem("vf_ready")
        gm_out = sem("gm_out")
        state_in = sem("state_in")
        state_out = sem("state_out")
        relu2_ready = sem("relu2_ready")
        hid_part_hi = sem("hid_part_hi")
        hid_ready = sem("hid_ready")
        xin_ready = sem("xin_ready")
        gelu_ready = sem("gelu_ready")
        gated_ready = sem("gated_ready")
        scanned = sem("scanned")
        y_rstd_ready = sem("y_rstd_ready")
        q_dec_ready = sem("q_dec_ready")
        xc_ready = sem("xc_ready")
        gate_landed = sem("gate_landed")
        tanh_ready = sem("tanh_ready")
        root_ready = sem("root_ready")
        lru_done = sem("lru_done")
        stored = sem("stored")
        passed = sem("passed")
        powers_used = sem("powers_used")
        act_exp = sem("act_exp")
        under_root = sem("under_root")
        act_step = sem("act_step")
        dve_step = sem("dve_step")

        def by_bank(t):
            return t.rearrange("p (c t) -> p c t", c=BANKS)

        def whole(s):
            return psum[:, s, :, 0:CH]

        def part(s, n):
            return psum[:, s, n // 3, n % 3 * P:(n % 3 + 1) * P]

        def chunk(t, n):
            return t[:, n * P:(n + 1) * P]

        def tile_of(t, k):
            return t[:, k, :] if isinstance(k, int) else t[:, ds(k, 1), :].rearrange("p a t -> p (a t)")

        def col(t, n):
            return t[:, n:n + 1] if isinstance(n, int) else t[:, ds(n, 1)]

        def at(i, per, c):
            return c if i is None else i * per + c

        def tokens(t):
            return ((t[:, 0:LAT], 0), (t[:, LAT:TOK], 1))

        LATC = LAT // CH
        LREST = LAT - LATC * CH

        def pieces(s, t):
            return (
                (psum[:, s, 0:LATC, 0:CH], t[:, 0:LATC * CH].rearrange("p (c t) -> p c t", c=LATC), 0),
                (psum[:, s, LATC, 0:LREST], t[:, LATC * CH:LAT], 0),
                (psum[:, s, LATC, LREST:CH], t[:, LAT:TOK], 1),
            )

        def item_out(eng, i, per, c):
            eng.wait_ge(read_out[c % 2], at(i, per // 2, c // 2 + 2))

        def square(n, k):
            return square_start[k % 2] if n == 0 else square_out if n in (1, 3) else square_mlp

        def gained(n, k):
            return gained_start[k % 2] if n == 0 else gained_out[k] if n in (1, 3) else gained_mlp

        par_loads = [(consts[:], a["consts"])] + [(par_rows[r % P:r % P + n, r // P, :], src) for r, n, src in (
            (R_MODB, 2 * MODS, a["mod_b"].rearrange("l (m p) -> (l m) p", p=P)),
            (R_NMIX, 2 * KT, a["norm_mix"].rearrange("l (m p) -> (l m) p", p=P)),
            (R_NMLP, 2 * KT, a["norm_mlp"].rearrange("l (m p) -> (l m) p", p=P)),
            (R_CONVW, 4 * KT, a["lru_conv_w"][0].rearrange("j (m p) -> (j m) p", p=P)),
            (R_CONVB, KT, a["lru_conv_b"][0].rearrange("(m p) -> m p", p=P)),
            (R_GA, 2 * KT, a["lru_gate_a_b"][0].rearrange("j (m p) -> (j m) p", p=P)),
            (R_GX, 2 * KT, a["lru_gate_x_b"][0].rearrange("j (m p) -> (j m) p", p=P)),
            (R_LAM, 2 * KT, a["lru_lambda"][0].rearrange("j (m p) -> (j m) p", p=P)),
            (R_LF, KT, a["state_lru_fwd"][0].rearrange("l (m p) -> (l m) p", p=P)),
            (R_LB, KT, a["state_lru_bwd"][0].rearrange("l (m p) -> (l m) p", p=P)),
            (R_FN, KT, a["final_norm"].rearrange("(m p) -> m p", p=P)),
            (R_C, KT, a["c"][0].rearrange("(m p) -> m p", p=P)),
            (R_C + KT, KT, a["c_ctx"].rearrange("(m p) -> m p", p=P)),
        )]
        par_loads += [
            (ws_rows[:], a["gmlp_ws"][0].rearrange("g p q -> p g q")),
            (dec_row[0:1, 0:HEADS], a["ret_decay_fwd"]), (dec_row[0:1, HEADS:2 * HEADS], a["ret_decay_bwd"]),
            (bs_row[0:1, :], a["gmlp_bs"].rearrange("e g p -> e (g p)")),
        ]

        block = ctx.enter_context(nc.Block())

        @block.sync
        def _(sp):
            sp.nop().then_inc(state_out, 32)
            for dst, src in par_loads[1::2]:
                sp.dma_start(dst, src).then_inc(par_landed[1], 16)
            for n in range(NCH):
                src = a["x_sample"][0, n * P:(n + 1) * P, :] if n < LCH else a["x_prompt"][0]
                sp.dma_start(x_rows[:, n, :], src).then_inc(x_landed[n], 16)

            def load_unit(i, per, c, src):
                sp.wait_ge(split_done, at(i, per, c + 1))
                sp.sem_inc(passed, 1)
                dst = w_raw[:, c % 2, :].rearrange("p (k m) -> p k m", k=src.shape[1])
                sp.dma_start(dst, src).then_inc(raw_landed[c % 2], 16)

            def load_mod(i, per, c, layer):
                src = cols(a["mod_w"][layer], at(i, per, c - layer * MODS) * P)
                for half in range(2):
                    sp.wait_ge(mod_summed, at(i, 2 * per, 2 * (c - FIRST_MODS) + half + 1))
                    sp.sem_inc(passed, 1)
                    sp.dma_start(mod_raw[:, half], src[:, half * KT // 2:(half + 1) * KT // 2, :]).then_inc(mod_landed[half], 16)

            def cols(w, start):
                w = w[:, start:start + P] if isinstance(start, int) else w[:, ds(sp.snap(start), P)]
                return w.rearrange("(k p) m -> p k m", p=P)

            def out_proj(l, w, mods=()):
                for c in range(KT):
                    load_unit(None, 0, AT_OUT[l].units + c, cols(w, c * P))
                    if c == 0:
                        for m in mods:
                            load_mod(None, 0, m, 0)
                    if c == 3:
                        sp.wait_ge(h_ready, H_MIX[l] + 3)
                        sp.dma_start(x[:, 0:3, :].rearrange("p k t -> p (k t)"), x_spill[:, 0:3 * TOK]).then_inc(x_back[0], 16)
                        sp.wait_ge(h_ready, H_MIX[l] + KT)
                        sp.dma_start(x[:, 3:KT, :].rearrange("p k t -> p (k t)"), x_spill[:, 3 * TOK:]).then_inc(x_back[1], 16)

            def mlp(l):
                u = AT_MLP[l].units
                with sp.Fori(0, GROUPS) as g:
                    for j in range(GRP):
                        load_unit(g, GRP_UNITS, u + j, cols(a["mlp_w1"][l], g * (GRP * P) + j * P))
                        if l == 0 and j > 1:
                            load_mod(g, GRP_MODS, MODS + j - 2, 1)
                    for j in range(GRP):
                        src = a["mlp_w2"][l][ds(sp.snap(g * (GRP * P)), GRP * P), j * 2 * P:(j + 1) * 2 * P]
                        load_unit(g, GRP_UNITS, u + GRP + j, src.rearrange("(k p) m -> p k m", p=P))
                        if l == 0:
                            load_mod(g, GRP_MODS, MODS + GRP + j - 2, 1)

            for k in range(KT):
                sp.dma_start(scale_raw[:, k, :], a["mod_w"][0][k * P:(k + 1) * P, SC1 * P:(SC1 + KT) * P]).then_inc(scale_landed[k], 16)
            load_unit(0, HEAD_UNITS, 0, cols(a["ab_w_in"][0], SECTIONS[0] * HD))
            sp.wait_ge(mini_done, 1)
            for k in range(KT):
                sp.dma_start(shift_raw[k][:], a["mod_w"][0][k * P:(k + 1) * P, SH1 * P:(SH1 + KT) * P]).then_inc(shift_landed[k], 16)
            sp.wait_ge(mini_done, START_ITEMS)
            sp.wait_ge(mod_used, FIRST_MODS)
            sp.dma_start(rope[:], a["rope"]).then_inc(rope_landed, 16)

            mods_behind = ((-2, -1), (0,), (1,), (2,), (3,), (4, 5))

            def head(h):
                for j, section in enumerate(SECTIONS):
                    if j or not isinstance(h, int):
                        load_unit(h, HEAD_UNITS, j, cols(a["ab_w_in"][0], h * P + section * HD))
                    if j == 2:
                        sp.wait_ge(unit_done, h * HEAD_UNITS + 1)
                        sp.dma_start(s0_fwd[:], a["state_ret_fwd"][0, 0, ds(h, 1)].rearrange("a d e -> (a d) e")).then_inc(state_in, 16)
                        sp.dma_start(chunk(s_bwd, LCH - 1), a["state_ret_bwd"][0, 0, ds(h, 1)].rearrange("a d e -> (a d) e")).then_inc(state_in, 16)
                    for m in mods_behind[j]:
                        if m >= 0 or not isinstance(h, int):
                            load_mod(h, HEAD_MODS, FIRST_MODS + m, 0)
                item_out(sp, h, HEAD_ITEMS, AT_MIX[0].items + 6)
                sp.dma_start(a["new_ret_bwd"][0, 0, ds(h, 1)].rearrange("a d e -> (a d) e"), chunk(s_bwd, LCH)).then_inc(state_out, 16)
                item_out(sp, h, HEAD_ITEMS, AT_MIX[0].items + 8)
                sp.dma_start(a["new_ret_fwd"][0, 0, ds(h, 1)].rearrange("a d e -> (a d) e"), chunk(k_bwd, LCH)).then_inc(state_out, 16)

            head(0)
            with sp.Fori(1, HEADS) as h:
                head(h)
            out_proj(0, a["ab_w_out"][0], [FIRST_MODS + HEADS * HEAD_MODS + m for m in mods_behind[0]])
            mlp(0)

            with sp.Fori(0, KT) as b:
                load_unit(b, BLK_UNITS, AT_MIX[1].units, cols(a["lru_w_in"][0], b * P + D_MODEL))
                load_unit(b, BLK_UNITS, AT_MIX[1].units + 1, cols(a["lru_w_in"][0], b * P))
                sp.wait_ge(mini_done, at(b, BLK_MINIS, AT_MIX[1].minis))
                for d in range(2):
                    for j, name in enumerate(("lru_gate_a_w", "lru_gate_x_w")):
                        src = a[name][0, d, ds(b, 1)].rearrange("a c d -> (a c) d")
                        sp.dma_start(gate_w[:, 2 * d + j, :], src).then_inc(gate_landed, 16)
            out_proj(1, a["lru_w_out"][0])
            mlp(1)

            sp.wait_ge(lru_done, 1 + KT)
            sp.dma_start(a["new_lru_fwd"][0, 0].rearrange("(b p) -> p b", p=P), lru_last[:, 0, :]).then_inc(stored, 16)
            sp.dma_start(a["new_lru_bwd"][0, 0].rearrange("(b p) -> p b", p=P), lru_last[:, 1, :]).then_inc(stored, 16)
            for n in range(NCH):
                item_out(sp, None, 0, AT_END.items + n)
                dst = a["y_sample"][0, n * P:(n + 1) * P, :] if n < LCH else a["y_prompt"][0]
                sp.dma_start(dst, y_rows[:, n, :]).then_inc(stored, 16)
            sp.wait_ge(stored, 16 * (NCH + 2))
            sp.wait_ge(state_out, 32 + 32 * HEADS)
            sp.wait_ge(x_spilled, 32)

        @block.gpsimd
        def _(pool):
            pool.nop().then_inc(split_done, 2)
            pool.memset(ones[:], 1.0).then_inc(ones_set, 1)
            pool.memset(eps[:], EPS).then_inc(ones_set, 1)

            def split(i, s):
                pool.wait_ge(raw_landed[s], at(i, 16, 16))
                if i is not None:
                    pool.wait_ge(unit_done, i * 2 + (s - 1))
                pool.sem_inc(passed, 1)
                pool.tensor_copy(w_hi[:, s, :], w_raw[:, s, :]).then_inc(hi_done, 1)
                pool.wait_ge(hi_done, at(i, 2, s + 1))
                pool.tensor_tensor(w_lo[:, s, :], w_raw[:, s, :], w_hi[:, s, :].bitcast(F32), ALU.subtract).then_inc(split_done, 1)

            def low_part(k):
                pool.wait_ge(part_hi, H_MIX[1] + k + 1)
                pool.tensor_tensor(h_lo[:, k, 0:TOK], mix[:, k, :], h_hi[:, k, 0:TOK].bitcast(F32), ALU.subtract).then_inc(h_ready, 1)

            def block_products(b, last):
                pool.wait_ge(xc_ready, b + 2)
                for d in range(2):
                    item_out(pool, b, BLK_ITEMS, AT_MIX[1].items + 3 + 2 * d)
                    pool.tensor_tensor(gated[d][:], gated[d][:], xc[:], ALU.mult).then_inc(gated_ready, 1)
                if last:
                    pool.wait_ge(h_ready, H_MIX[1] + DVE_LOW)
                    for k in range(DVE_LOW, KT - 1):
                        low_part(k)

            first = AT_MIX[1].units // 2 + 1
            split(None, 0)
            split(None, 1)
            with pool.Fori(1, first) as i:
                split(i, 0)
                split(i, 1)
            with pool.Fori(0, KT - 1) as b:
                split(b + first, 0)
                split(b + first, 1)
                block_products(b, False)
            split(first + KT - 1, 0)
            split(first + KT - 1, 1)
            block_products(KT - 1, True)
            with pool.Fori(first + KT, UNITS // 2) as i:
                split(i, 0)
                split(i, 1)

        @block.tensor
        def _(pe):
            pe.nop().then_inc(read_out[0], 1)
            pe.nop().then_inc(read_out[1], 1)

            def take_set(i, per, c):
                pe.wait_ge(read_out[c % 2], at(i, per // 2, c // 2 + 1))
                return c % 2

            def three_passes(s, tiles, hi, lo, in_hi, in_lo, width=TOK, first=True, last=True, before=None, behind=None):
                for n, k in enumerate(tiles):
                    if before:
                        before(n)
                    for w, v in ((hi[k], in_hi), (hi[k], in_lo), (lo[k], in_hi)):
                        for c in range(BANKS):
                            end = width if c == BANKS - 1 else (c + 1) * CH
                            mm = pe.matmul(psum[:, s, c, 0:end - c * CH], w, v[:, k, c * CH:end],
                                           start=(first and n == 0 and w is hi[k] and v is in_hi),
                                           stop=(last and n == len(tiles) - 1 and w is lo[k]))
                    if behind:
                        behind(n)
                return mm

            def parts(w, c, n, start=0):
                view = w[:, c % 2, :].rearrange("p (k m) -> p k m", k=n)
                return [view[:, k, start:start + P] for k in range(n)]

            def project(i, items, item, per, unit, before=None, behind=None, width=COLS):
                s = take_set(i, items, item)
                pe.wait_ge(split_done, at(i, per, unit + 3))
                return three_passes(s, range(KT), parts(w_hi, unit, KT), parts(w_lo, unit, KT), h_hi, h_lo, width,
                                    before=before, behind=behind)

            def mod_column(i, per, c):
                pe.wait_ge(mod_summed, at(i, 2 * per, 2 * (c - FIRST_MODS) + 4))
                start = at(i, 2 * per, 2 * c)
                for n in range(2):
                    dst = mod_psum[:, start + n:start + n + 1] if isinstance(start, int) else mod_psum[:, ds(start + n, 1)]
                    last = pe.matmul(dst, mod_sum[:, c % 2, n, :], ones[:, 0:1], start=True, stop=True)
                last.then_inc(mod_used, 1)

            def turn(s, t):
                for n in range(NCH):
                    last = pe.transpose(part(s, n), chunk(t, n), ident[:])
                return last

            def norm_waits(n):
                def before(k):
                    pe.wait_ge(h_ready, H_NORM[n] + k + 1)

                def behind(k):
                    c = k - (KT - BANKS)
                    if c < 0:
                        return
                    if c == 0:
                        pe.wait_ge(sq_added, (KT - 1) * (n + 1))
                    if BANKS * n + c:
                        pe.wait_ge(ssq_read, BANKS * n + c)
                    pe.matmul(ssq_psum[:, 0:CH], ones[:], sumsq[:, c * CH:(c + 1) * CH], start=True, stop=True).then_inc(ssq_done, 1)

                return before, behind

            pe.wait_ge(ones_set, 2)
            for n in range(2):
                pe.wait_ge(par_landed[n], 16 * len(par_loads[n::2]))
            s = take_set(None, 0, 0)
            for n in range(2):
                pe.transpose(psum[:, s, 0, n * P:(n + 1) * P], par_rows[:, n, :], consts[:, C_ID:C_ID + P])
            for n in range(HEADS):
                pe.transpose(psum[:, s, 1 + n // 2, n % 2 * P:(n % 2 + 1) * P], ws_rows[:, n, :], consts[:, C_ID:C_ID + P])
            pe.matmul(psum[:, s, 0, 2 * P:2 * P + 2 * HEADS], ones[0:1, :], dec_row[0:1, :], start=True, stop=True)
            for n in range(2):
                last = pe.matmul(psum[:, s, 1 + n, 2 * P:4 * P], ones[0:1, :], bs_row[0:1, n * 2 * P:(n + 1) * 2 * P],
                                 start=True, stop=True)
            last.then_inc(mini_done, 1)
            for n in range(NCH):
                s = take_set(None, 0, 1 + n)
                pe.wait_ge(x_landed[n], 16)
                for k in range(KT):
                    last = pe.transpose(psum[:, s, k // 4, k % 4 * P:(k % 4 + 1) * P], x_rows[:, n, k * P:(k + 1) * P],
                                        consts[:, C_ID:C_ID + P])
                last.then_inc(mini_done, 1)

            def first_rows(item, landed, weights):
                s = take_set(None, 0, item)
                for k in range(KT):
                    pe.wait_ge(landed[k], 16)
                    for c in range(2):
                        last = pe.matmul(psum[0:2, s, c, :], cond[:, :, k], weights(k)[:, c * 512:(c + 1) * 512],
                                         start=(k == 0), stop=(k == KT - 1))
                last.then_inc(mini_done, 1)

            def first_columns(item, n, tile):
                item_out(pe, None, 0, item)
                for m in range(KT):
                    at_column = 2 * (tile + m)
                    last = pe.transpose(mod_psum[:, at_column:at_column + 2], mod_rows[0:2, n, m * P:(m + 1) * P], consts[0:2, C_ID:C_ID + 2])
                last.then_inc(mod_used, KT)

            pe.wait_ge(cond_ready, 1)
            first_rows(SCALE_ITEM, scale_landed, lambda k: scale_raw[:, k, :])
            first_columns(SCALE_ITEM, 0, SC1)
            first_rows(SHIFT_ITEM, shift_landed, lambda k: shift_raw[k])

            I0, U0 = AT_MIX[0].items, AT_MIX[0].units
            M0 = FIRST_MODS

            def head(h):
                def big(item, unit):
                    if not isinstance(h, int) or unit > 0:
                        return project(h, HEAD_ITEMS, I0 + item, HEAD_UNITS, U0 + unit)
                    tile_ready, sum_squares = norm_waits(0)

                    def before(k):
                        if k == 2:
                            pe.wait_ge(mod_read, 1)
                            first_columns(SHIFT_ITEM, 1, SH1)
                        tile_ready(k)

                    project(None, 0, I0, 0, U0, before, sum_squares, TOK)
                    pe.wait_ge(shift_ready, 1)
                    hi, lo = parts(w_hi, U0, KT), parts(w_lo, U0, KT)
                    for k in range(KT):
                        for w, v in ((hi[k], h_hi), (hi[k], h_lo), (lo[k], h_hi)):
                            last = pe.matmul(psum[:, I0 % 2, BANKS - 1, CH:CH + 2], w, v[:, k, TOK:COLS],
                                             start=(k == 0 and w is hi[k] and v is h_hi), stop=(k == KT - 1 and w is lo[k]))
                    return last

                def mini(item):
                    return take_set(h, HEAD_ITEMS, I0 + item)

                def mod_col(c):
                    if c == 0:
                        pe.wait_ge(mod_read, h + FIRST_BATCHES)
                    mod_column(h, HEAD_MODS, M0 + c)

                big(0, 0).then_inc(unit_done, 1)
                big(1, 1).then_inc(unit_done, 1)
                mod_col(0)
                s = mini(2)
                pe.wait_ge(k_ready, h + 1)
                turn(s, kT).then_inc(mini_done, 1)
                big(3, 2).then_inc(unit_done, 1)
                mod_col(1)
                s = mini(4)
                pe.wait_ge(activated, at(h, HEAD_UNITS, 2))
                turn(s, v_raw).then_inc(mini_done, 1)
                mod_col(2)
                big(5, 3).then_inc(unit_done, 1)
                mod_col(3)
                s = mini(6)
                for n in range(NCH):
                    last = pe.matmul(part(s, n), chunk(k_bwd, n), chunk(v_row, n), start=True, stop=True)
                last.then_inc(mini_done, 1)
                s = mini(7)
                pe.wait_ge(q_ready, h + 1)
                for n in range(NCH):
                    last = pe.matmul(part(s, n), chunk(kT, n), chunk(qT, n), start=True, stop=True)
                last.then_inc(mini_done, 1)
                s = mini(8)
                for n in range(NCH):
                    last = pe.matmul(part(s, n), chunk(k_fwd, n), chunk(v_row, n), start=True, stop=True)
                last.then_inc(mini_done, 1)
                big(9, 4).then_inc(unit_done, 1)
                mod_col(4)
                s = mini(10)
                pe.wait_ge(activated, at(h, HEAD_UNITS, 4))
                turn(s, v_raw).then_inc(mini_done, 1)
                s = mini(11)
                item_out(pe, h, HEAD_ITEMS, I0 + 8)
                for n in range(NCH):
                    last = pe.matmul(part(s, n), chunk(probs, n), chunk(v_row, n), start=True, stop=(n == LCH))
                    if n < LCH:
                        state = s0_fwd[:] if n == 0 else chunk(k_bwd, n)
                        pe.matmul(part(s, n), chunk(turned, n), state, start=False, stop=False)
                        last = pe.matmul(part(s, n), chunk(swapped, n), chunk(s_bwd, n), start=False, stop=True)
                last.then_inc(mini_done, 1)
                mod_col(5)
                s = mini(12)
                pe.wait_ge(activated, at(h, HEAD_UNITS, 5))
                turn(s, kT).then_inc(mini_done, 1)
                big(13, 5).then_inc(unit_done, 1)
                mod_col(6)
                s = mini(14)
                pe.wait_ge(o_ready, h + 1)
                turn(s, v_raw).then_inc(mini_done, 1)
                s = mini(15)
                pe.wait_ge(vf_ready, h + 1)
                for n in range(NCH):
                    last = pe.matmul(part(s, n), chunk(kT, n), tile_of(wsT, h), start=True, stop=True)
                last.then_inc(mini_done, 1)
                mod_col(7)

            def out_proj(l):
                order, late = MIX_ORDER[l], LATE[l]
                I, U = AT_OUT[l].items, AT_OUT[l].units
                spans = ((order[:KT - late], True), (order[KT - late:], False))
                for tiles, early in spans:
                    for c in range(2):
                        if early:
                            take_set(None, 0, I + c)
                            pe.wait_ge(split_done, U + c + 3)

                        def tile_ready(n):
                            if c == 0:
                                pe.wait_ge(h_ready, H_MIX[l] + n + (1 if early else KT - late + 1))

                        mm = three_passes((I + c) % 2, tiles, parts(w_hi, U + c, KT), parts(w_lo, U + c, KT), h_hi, h_lo,
                                          first=early, last=not early, before=tile_ready)
                        if not early:
                            mm.then_inc(unit_done, 1)
                for c in range(2, KT):
                    project(None, 0, I + c, 0, U + c, width=TOK).then_inc(unit_done, 1)

            def mlp(l):
                I, U = AT_MLP[l].items, AT_MLP[l].units

                def group(g):
                    def mod_col(c):
                        if l == 0:
                            if c == 0:
                                pe.wait_ge(mod_read, g + (FIRST_BATCHES + HEADS))
                            mod_column(g, GRP_MODS, MODS + c)

                    for j in range(GRP):
                        waits = norm_waits(2 * l + 1) if isinstance(g, int) and g == 0 and j == 0 else (None, None)
                        project(g, GRP_ITEMS, I + j, GRP_UNITS, U + j, *waits).then_inc(unit_done, 1)
                        if j:
                            mod_col(j - 1)

                    def second(unit, half, tiles, **kw):
                        return three_passes((I + GRP + half) % 2, tiles, parts(w_hi, unit, GRP, half * P),
                                            parts(w_lo, unit, GRP, half * P), hid_hi, hid_lo, **kw)

                    hidden = BANKS * GRP * GROUPS * l
                    for half in range(2):
                        take_set(g, GRP_ITEMS, I + GRP + half)
                        if half == 0:
                            pe.wait_ge(split_done, at(g, GRP_UNITS, U + GRP + 3))
                            pe.wait_ge(hid_ready, at(g, BANKS * GRP, hidden + BANKS * (GRP - 1) + 1))
                        second(U + GRP, half, range(GRP - 1), last=False)
                    pe.wait_ge(hid_ready, at(g, BANKS * GRP, hidden + BANKS * GRP + 1))
                    for half in range(2):
                        second(U + GRP, half, (GRP - 1,), first=False).then_inc(unit_done if half else mini_done, 1)
                    mod_col(3)
                    for j in range(1, GRP):
                        unit = U + GRP + j
                        for half in range(2):
                            take_set(g, GRP_ITEMS, I + GRP + 2 * j + half)
                            if half == 0:
                                pe.wait_ge(split_done, at(g, GRP_UNITS, unit + 3))
                            second(unit, half, range(GRP)).then_inc(unit_done if half else mini_done, 1)
                        if j > 1:
                            mod_col(2 + j)

                group(0)
                with pe.Fori(1, GROUPS) as g:
                    group(g)

            head(0)
            with pe.Fori(1, HEADS) as h:
                head(h)
            out_proj(0)
            mlp(0)

            I1, U1 = AT_MIX[1].items, AT_MIX[1].units

            def lru_block(b):
                waits = norm_waits(2) if isinstance(b, int) else (None, None)
                project(b, BLK_ITEMS, I1, BLK_UNITS, U1, *waits).then_inc(unit_done, 1)
                project(b, BLK_ITEMS, I1 + 1, BLK_UNITS, U1 + 1).then_inc(unit_done, 1)
                for j in range(4):
                    s = take_set(b, BLK_ITEMS, I1 + 2 + j)
                    if j == 0:
                        pe.wait_ge(gate_landed, at(b, 64, 64))
                        pe.wait_ge(xc_ready, b + 2)
                    for c in range(BANKS):
                        last = pe.matmul(psum[:, s, c, 0:CH], gate_w[:, j, :], xc[:, c * CH:(c + 1) * CH], start=True, stop=True)
                    last.then_inc(mini_done, 1)

            lru_block(0)
            with pe.Fori(1, KT) as b:
                lru_block(b)
            out_proj(1)
            mlp(1)

            pe.wait_ge(gained_ready, 5 * KT)
            for n in range(NCH):
                s = take_set(None, 0, AT_END.items + n)
                for k in range(KT):
                    last = pe.transpose(psum[:, s, k // 4, k % 4 * P:(k % 4 + 1) * P], y_cols[:, k, n * P:(n + 1) * P], ident[:])
                last.then_inc(mini_done, 1)
                if n == 0:
                    pe.wait_ge(sq_added, (KT - 1) * 5)
                    for m in range(NCH):
                        last = pe.matmul(ssq_psum[:, m:m + 1], chunk(sumsq, m), ones[:, 0:1], start=True, stop=True)
                    last.then_inc(ssq_done, 1)

        @block.scalar
        def _(act):
            steps = Steps()
            for dst, src in par_loads[::2]:
                act.dma_start(dst, src).then_inc(par_landed[0], 16)

            item_out(act, None, 0, 0)
            act.activation(cond[:].rearrange("p c k -> p (c k)"), par[:, R_C:R_C + 2 * KT], ACT.Silu).then_inc(cond_ready, 1)
            act.wait_ge(neg_abs_ready, 1)
            act.activation(sp_exp[:], sp_neg[:], ACT.Exp).then_inc(exp_ready, 1)
            for n in range(NCH):
                s = (1 + n) % 2
                act.wait_ge(mini_done, 2 + n)
                act.activation(x[:, :, n * P:(n + 1) * P], psum[:, s, 0:2, :].rearrange("p b (k t) -> p (b k) t", k=4),
                               ACT.Copy).then_inc(read_out[s], 1)
            def square_tile(n, k):
                places = 2 if n == 0 else 1
                if k > places:
                    act.wait_ge(sq_added, n * (KT - 1) + k - places)
                dst = sumsq if k == 0 else square(n, k)
                act.activation(dst[:], x[:, k, :], ACT.Square).then_inc(sq_ready, 1)

            def gain_tile(n, k):
                m = gained(n, k)
                if k == 0:
                    act.wait_ge(gain_ready, n + 1)
                if n == 0 and k >= 2:
                    act.wait_ge(h_ready, H_NORM[0] + k - 1)
                if n == 2 and k >= 1:
                    act.wait_ge(h_ready, H_NORM[2] + k)
                for t, c in tokens(x[:, k, :]):
                    start = c * LAT
                    last = act.activation(m[:, start:start + t.shape[1]], t, ACT.Copy, scale=gain[:, k, c:c + 1])
                if n:
                    last = act.activation(m[:, TOK:COLS], mod[:, n // 2, (SH1, SH2)[n % 2] + k, :], ACT.Copy)
                last.then_inc(gained_ready, 1)

            def high_part(n, k):
                act.wait_ge(gained_ready, n * KT + k + 1)
                act.activation(h_hi[:, k, :], gained(n, k)[:], ACT.Copy).then_inc(part_hi, 1)

            def roots(n):
                for c in range(BANKS):
                    act.wait_ge(ssq_done, BANKS * n + c + 1)
                    act.activation(rstd[:, c * CH:(c + 1) * CH], ssq_psum[:, 0:CH], ACT.Sqrt, bias=eps[:],
                                   scale=1.0 / D_MODEL).then_inc(ssq_read, 1)

            def biased(t, b, func, scale=1.0):
                for v, c in tokens(t):
                    last = act.activation(v, v, func, bias=bias[:, b, c:c + 1], scale=scale)
                return last

            def out_proj(l):
                act.wait_ge(unit_done, AT_OUT[l].units)
                for n, k in enumerate(MIX_ORDER[l]):
                    if l == 1 and n < KT - 1:
                        continue
                    if l == 0 and k == 3:
                        item_out(act, None, 0, AT_OUT[0].items - 2)
                    if l == 0 and k in (0, 7):
                        act.wait_ge(gm_out, HEADS + (1 if k else 0))
                    if l == 1:
                        act.wait_ge(lru_done, 1 + KT)
                    act.activation(h_hi[:, k, 0:TOK], mix[:, k, :], ACT.Copy).then_inc(part_hi, 1)
                norm = 2 * l + 1
                for k in range(KT - 1):
                    item_out(act, None, 0, AT_OUT[l].items + k)
                    gain_tile(norm, k)
                    square_tile(norm, k)
                act.wait_ge(unit_done, AT_MLP[l].units)
                for k in range(KT):
                    if k == 4:
                        item_out(act, None, 0, AT_OUT[l].items + KT - 1)
                        gain_tile(norm, KT - 1)
                        square_tile(norm, KT - 1)
                    high_part(norm, k)
                roots(norm)

            def mlp(l):
                I, U, M = AT_MLP[l].items, AT_MLP[l].units, AT_MLP[l].minis

                def group(g):
                    for j in range(GRP):
                        chunks = BANKS * (l * GRP * GROUPS + j)
                        for c in range(BANKS):
                            t = slice(c * CH, (c + 1) * CH)
                            if c < BANKS - 1:
                                act.wait_ge(scaled, at(g, 2 * GRP, 2 * (l * GRP * GROUPS + j) + c + 1))
                                act.activation(relu[:, t], relu[:, t], ACT.Relu, bias=bias[:, j, 0:1]).then_inc(relu_ready, 1)
                            else:
                                item_out(act, g, GRP_ITEMS, I + j)
                                act.activation(relu[:, c * CH:LAT], relu[:, c * CH:LAT], ACT.Relu, bias=bias[:, j, 0:1])
                                act.activation(relu[:, LAT:TOK], relu[:, LAT:TOK], ACT.Relu, bias=bias[:, j, 1:2]).then_inc(relu_ready, 1)
                        for c in range(BANKS):
                            t = slice(c * CH, (c + 1) * CH)
                            act.wait_ge(relu2_ready, at(g, BANKS * GRP, chunks + c + 2))
                            act.activation(hid_hi[:, j, t], relu2[:, t], ACT.Copy).then_inc(hid_part_hi, 1)

                with act.Fori(0, GROUPS - 1) as g:
                    group(g)
                group(GROUPS - 1)
                norm = 2 * l + 2
                for k in range(KT):
                    item_out(act, None, 0, I + (GROUPS - 1) * GRP_ITEMS + GRP + k)
                    if l == 0:
                        gain_tile(norm, k)
                        high_part(norm, k)
                    else:
                        act.activation(y_cols[:, k, :], x[:, k, :], ACT.Copy, scale=par[:, R_FN + k:R_FN + k + 1]).then_inc(gained_ready, 1)
                    square_tile(norm, k)
                if l == 0:
                    roots(norm)

            for n in (NCH, NCH - 1):
                item_out(act, None, 0, n)
            for k in range(KT):
                square_tile(0, k)
            act.wait_ge(decays_ready, 2)
            for n in range(HEADS):
                log_f, log_b = lg[:, n:n + 1], lg[:, HEADS + n:HEADS + n + 1]
                act.activation(exps[:, 0, n, :], consts[:, C_DF:C_DF + P], ACT.Exp, scale=log_f)
                act.activation(exps[:, 1, n, :], consts[:, C_DB:C_DB + P], ACT.Exp, scale=log_b)
                act.activation(k_dec[:, 0, n:n + 1], consts[:, C_KF:C_KF + 1], ACT.Exp, scale=log_f)
                act.activation(k_dec[:, 1, n:n + 1], consts[:, C_KB:C_KB + 1], ACT.Exp, scale=log_b)
            act.activation(g_chunk[:].rearrange("p d h -> p (d h)"), lg[:], ACT.Exp, scale=float(P)).then_inc(powers_ready, 1)
            for k in range(KT):
                gain_tile(0, k)
            roots(0)
            act.wait_ge(powers_used, 1)

            def spill(norm):
                act.wait_ge(h_ready, H_NORM[norm] + KT)
                act.wait_ge(sq_added, (norm + 1) * (KT - 1))
                act.dma_start(x_spill, x[:].rearrange("p k t -> p (k t)")).then_inc(x_spilled, 16)

            spill(0)
            I0, U0, M0 = AT_MIX[0].items, AT_MIX[0].units, AT_MIX[0].minis
            with act.Fori(0, HEADS) as h:
                steps.enter(h, 9)

                def mini(n):
                    act.wait_ge(mini_done, at(h, HEAD_MINIS, M0 + n + 1))

                def swap():
                    for q in range(4):
                        last = act.activation(swapped[32 * q:32 * q + 32, 0:LAT],
                                              turned[32 * (q ^ 1):32 * (q ^ 1) + 32, 0:LAT], ACT.Copy)
                    return last

                item_out(act, h, HEAD_ITEMS, I0)
                biased(turned, 0, ACT.Identity, float(P) ** -0.5).then_inc(activated, 1)
                act.wait_ge(activated, at(h, HEAD_UNITS, 1))
                swap().then_inc(projected, 1)
                item_out(act, h, HEAD_ITEMS, I0 + 1)
                biased(v_raw, 1, ACT.Identity).then_inc(activated, 1)
                item_out(act, h, HEAD_ITEMS, I0 + 3)
                biased(turned, 2, ACT.Identity).then_inc(activated, 1)
                act.wait_ge(activated, at(h, HEAD_UNITS, 3))
                swap().then_inc(projected, 1)
                mini(1)
                s = (I0 + 4) % 2
                act.activation(by_bank(v_row[:]), whole(s), ACT.Copy).then_inc(read_out[s], 1)
                act.activation(q_dec[:, 0, :], q_rows[:, 0, :], ACT.Exp, scale=col(lg, h))
                act.activation(q_dec[:, 1, :], q_rows[:, 1, :], ACT.Exp, scale=col(lg, h + HEADS)).then_inc(q_dec_ready, 1)
                item_out(act, h, HEAD_ITEMS, I0 + 5)
                biased(v_raw, 3, ACT.Silu).then_inc(activated, 1)
                item_out(act, h, HEAD_ITEMS, I0 + 9)
                biased(kT, 4, ACT.Gelu_apprx_tanh).then_inc(activated, 1)
                mini(5)
                s = (I0 + 10) % 2
                act.activation(by_bank(qT[:]), whole(s), ACT.Copy).then_inc(read_out[s], 1)
                act.wait_ge(o_var, h + 1)
                act.activation(row_rstd[:], mean_var[:, :, 1], ACT.Sqrt, bias=eps[:]).then_inc(o_root, 1)
                mini(7)
                s = (I0 + 12) % 2
                act.activation(by_bank(kT[:]), whole(s), ACT.Copy).then_inc(read_out[s], 1)
                item_out(act, h, HEAD_ITEMS, I0 + 12)
                for n in range(NCH):
                    act.activation(chunk(turned, n), chunk(kT, n), ACT.Square, accum_out=vf_sum[:, n:n + 1]).then_inc(act_step, 1)
                    summed = steps.done()
                act.wait_ge(act_step, summed)
                act.activation(vf_rstd[:], vf_sum[:], ACT.Sqrt, bias=eps[:], scale=1.0 / P).then_inc(vf_root, 1)
                item_out(act, h, HEAD_ITEMS, I0 + 13)
                biased(k_fwd, 5, ACT.Gelu_apprx_tanh).then_inc(activated, 1)
                mini(8)
                act.wait_ge(x_spilled, 16)
                s = (I0 + 14) % 2
                act.activation(by_bank(tile_of(mix, h)), whole(s), ACT.Copy).then_inc(read_out[s], 1)
            steps.leave(HEADS)
            out_proj(0)
            mlp(0)
            spill(2)

            I0, U0, M0 = AT_MIX[1].items, AT_MIX[1].units, AT_MIX[1].minis

            def conv_bias(i, n):
                item_out(act, i, BLK_ITEMS, I0 + n * BLK_ITEMS)
                for c, (start, size) in enumerate(((LPAD, LAT), (CTX0 + LPAD, CTX))):
                    t = xin[:, start:start + size]
                    last = act.activation(t, t, ACT.Identity, bias=bias[:, 0, c:c + 1])
                last.then_inc(xin_ready, 1)

            def lru_block(b, last_block):
                for j in range(4):
                    d, kind = j // 2, j % 2
                    s = (I0 + 2 + j) % 2
                    if kind == 0:
                        act.wait_ge(scanned, at(b, 2, d + 1))
                    act.wait_ge(mini_done, at(b, BLK_MINIS, M0 + j + 1))
                    act.activation(by_bank((gated if kind else rate)[d][:]), whole(s), ACT.Sigmoid,
                                   bias=col(par, b + ((R_GX if kind else R_GA) + d * KT))).then_inc(read_out[s], 1)
                act.wait_ge(lru_done, b + 1)
                for d in range(2):
                    item_out(act, b, BLK_ITEMS, I0 + 2 + 2 * d)
                    act.activation(work[d][:], rate[d][:], ACT.Exp, scale=col(lru_fall, b + d * KT)).then_inc(act_exp, 1)
                    act.activation(rate[d][:], rate[d][:], ACT.Tanh, scale=col(lru_rate, b + d * KT)).then_inc(tanh_ready, 1)
                for d in range(2):
                    act.wait_ge(under_root, at(b, 2, d + 1))
                    act.activation(work[d][:], work[d][:], ACT.Sqrt, scale=-1.0).then_inc(root_ready, 1)
                if not last_block:
                    conv_bias(b, 1)
                item_out(act, b, BLK_ITEMS, I0 + 1)
                for src, dst in zip(tokens(gate_raw), tokens(gelu_gate)):
                    last = act.activation(dst[0], src[0], ACT.Gelu_apprx_tanh, bias=bias[:, 1, src[1]:src[1] + 1])
                last.then_inc(gelu_ready, 1)

            conv_bias(None, 0)
            with act.Fori(0, KT - 1) as b:
                lru_block(b, False)
            lru_block(KT - 1, True)
            out_proj(1)
            mlp(1)
            act.wait_ge(ssq_done, BANKS * 4 + 1)
            act.activation(y_rstd[:], ssq_psum[:, 0:NCH], ACT.Sqrt, bias=eps[:], scale=1.0 / D_MODEL).then_inc(ssq_read, 1)
            act.wait_ge(y_rstd_ready, 1)
            for n in range(0, NCH, 2):
                s = (AT_END.items + n) % 2
                act.wait_ge(mini_done, AT_END.minis + n + 1)
                act.activation(y_rows[:, n, :].rearrange("p (k t) -> p k t", k=KT),
                               psum[:, s, 0:2, :].rearrange("p b (k t) -> p (b k) t", k=4), ACT.Copy,
                               scale=y_rstd[:, n:n + 1]).then_inc(read_out[s], 1)

        @block.vector
        def _(dve):
            steps = Steps()

            def after(value):
                dve.wait_ge(dve_step, value)

            for start_at_one in (relu2_ready, hid_ready, gm_out, lru_done):
                dve.nop().then_inc(start_at_one, 1)
            dve.nop().then_inc(mod_summed, 2)
            dve.nop().then_inc(scanned, 2)
            dve.wait_ge(mini_done, 1)
            dve.tensor_copy(par[:], psum[:, 0, 0, 0:2 * P])
            dve.tensor_copy(wsT[:].rearrange("p (b g) t -> p b (g t)", b=2), psum[:, 0, 1:3, 0:2 * P])
            dve.tensor_copy(bs_all[:].rearrange("p (b g) t -> p b (g t)", b=2), psum[:, 0, 1:3, 2 * P:4 * P])
            dve.tensor_copy(sp_z[:, 2 * HEADS:24], psum[:, 0, 0, R_LAM:R_LAM + 2 * KT])
            dve.tensor_copy(sp_z[:, 0:2 * HEADS], psum[:, 0, 0, 2 * P:2 * P + 2 * HEADS]).then_inc(read_out[0], 1)
            dve.tensor_copy(ident[:], consts[:, C_ID:C_ID + P])
            dve.tensor_copy(q_rows[:].rearrange("p d t -> p (d t)"), consts[:, C_QF:C_QF + 2 * P])
            item_out(dve, None, 0, 0)
            dve.tensor_scalar(sp_neg[:], sp_z[:], -1.0, None, ALU.mult).then_inc(dve_step, 1)
            after(steps.done())
            dve.tensor_scalar(sp_max[:], sp_neg[:], 0.0, None, ALU.max).then_inc(dve_step, 1)
            after(steps.done())
            dve.tensor_tensor(sp_neg[:], sp_neg[:], sp_z[:], ALU.min).then_inc(neg_abs_ready, 1)
            dve.wait_ge(exp_ready, 1)
            dve.tensor_scalar(sp_r[:], sp_exp[:], 2.0, None, ALU.add).then_inc(dve_step, 1)
            after(steps.done())
            dve.reciprocal(sp_r[:], sp_r[:]).then_inc(dve_step, 1)
            after(steps.done())
            dve.tensor_tensor(sp_r[:], sp_exp[:], sp_r[:], ALU.mult).then_inc(dve_step, 1)
            after(steps.done())
            dve.tensor_tensor(sp_r2[:], sp_r[:], sp_r[:], ALU.mult).then_inc(dve_step, 1)
            after(steps.done())
            dve.tensor_scalar(sp_q[:], sp_r2[:], 1.0 / 15, None, ALU.mult).then_inc(dve_step, 1)
            after(steps.done())
            for odd in (13, 11, 9, 7, 5, 3):
                dve.scalar_tensor_tensor(out=sp_q[:], in0=sp_q[:], scalar=1.0 / odd, in1=sp_r2[:],
                                         op0=ALU.add, op1=ALU.mult).then_inc(dve_step, 1)
                after(steps.done())
            dve.scalar_tensor_tensor(out=sp_q[:], in0=sp_q[:], scalar=1.0, in1=sp_r[:], op0=ALU.add, op1=ALU.mult).then_inc(dve_step, 1)
            after(steps.done())
            dve.scalar_tensor_tensor(out=sp_q[:], in0=sp_q[:], scalar=2.0, in1=sp_max[:], op0=ALU.mult, op1=ALU.add).then_inc(dve_step, 1)
            after(steps.done())
            dve.tensor_scalar(lru_rate[:], sp_q[:, 2 * HEADS:24], LRU_C / 2, None, ALU.mult)
            dve.tensor_scalar(lru_fall[:], sp_q[:, 2 * HEADS:24], -LRU_C, None, ALU.mult).then_inc(decays_ready, 1)
            dve.tensor_scalar(lg[:], sp_q[:, 0:2 * HEADS], -1.0, None, ALU.mult).then_inc(decays_ready, 1)

            def add_square(n, k):
                dve.wait_ge(sq_ready, n * KT + k + 1)
                if k > 1:
                    dve.wait_ge(sq_added, n * (KT - 1) + k - 1)
                dve.tensor_tensor(sumsq[:], sumsq[:], square(n, k)[:], ALU.add).then_inc(sq_added, 1)

            for k in range(1, KT):
                add_square(0, k)
            def mods_out(l, first, count, used):
                dve.wait_ge(mod_used, used)
                if isinstance(first, int):
                    dst, src = mod[:, l, first:first + count, :], mod_psum[:, (l * MODS + first) * 2:(l * MODS + first + count) * 2]
                    offset = par[:, R_MODB + l * MODS + first:R_MODB + l * MODS + first + count]
                else:
                    dst, src = mod[:, l, ds(first, count), :], mod_psum[:, ds(first * 2 + 2 * l * MODS, 2 * count)]
                    offset = par[:, ds(first + (R_MODB + l * MODS), count)]
                dve.tensor_tensor(dst, src.rearrange("p (m c) -> p m c", c=2), offset.unsqueeze(2).to_broadcast([P, count, 2]),
                                  ALU.add).then_inc(mod_read, 1)

            def sum_mod(i, per, c):
                dve.wait_ge(mod_used, at(i, per, c - 1))
                for half in range(2):
                    dve.wait_ge(mod_landed[half], at(i, 16 * per, 16 * (c - FIRST_MODS + 1)))
                    for k in range(KT // 2):
                        for n in range(2):
                            w, total = mod_raw[:, half, k, :], mod_sum[:, c % 2, n, :]
                            s = cond[:, n, half * KT // 2 + k:half * KT // 2 + k + 1]
                            if half + k == 0:
                                op = dve.tensor_scalar(total, w, s, None, ALU.mult)
                                op.then_inc(dve_step, 1)
                                done = steps.done()
                            else:
                                after(chain[n])
                                op = dve.scalar_tensor_tensor(out=total, in0=w, scalar=s, in1=total, op0=ALU.mult, op1=ALU.add)
                                if k == KT // 2 - 1 and n == 1:
                                    op.then_inc(mod_summed, 1)
                                    done = None
                                else:
                                    op.then_inc(dve_step, 1)
                                    done = steps.done()
                            chain[n] = done
                    if half == 0:
                        dve.wait_ge(mod_summed, at(i, 2 * per, 2 * (c - FIRST_MODS) + 3))
                        chain[1] = chain[0]

            chain = [None, None]

            def gains(n, batches):
                l, scale, row = n // 2, (SC1, SC2)[n % 2], (R_NMIX, R_NMLP)[n % 2]
                dve.wait_ge(mod_read, batches)
                dve.scalar_tensor_tensor(out=gain[:], in0=mod[:, l, scale:scale + KT, :], scalar=1.0,
                                         in1=par[:, row + l * KT:row + (l + 1) * KT].unsqueeze(2).to_broadcast([P, KT, 2]),
                                         op0=ALU.add, op1=ALU.mult).then_inc(gain_ready, 1)

            def low_part(k, of, before, n, width=COLS):
                dve.wait_ge(part_hi, before + n + 1)
                dve.tensor_tensor(h_lo[:, k, 0:width], of, h_hi[:, k, 0:width].bitcast(F32), ALU.subtract).then_inc(h_ready, 1)

            def reciprocals(n):
                for c in range(BANKS):
                    dve.wait_ge(ssq_read, BANKS * n + c + 1)
                    t = rstd[:, c * CH:(c + 1) * CH]
                    dve.reciprocal(t, t).then_inc(rstd_ready, 1)
                dve.wait_ge(rstd_ready, BANKS * (n + 1))

            def scale_out(s, b, dst, factor=None):
                shifts = psum[:, s, BANKS - 1, CH:CH + 2]
                if factor is None:
                    dve.tensor_copy(bias[:, b, :], shifts)
                else:
                    dve.tensor_scalar(bias[:, b, :], shifts, factor, None, ALU.mult)
                return dve.tensor_tensor(by_bank(dst[:]), whole(s), by_bank(rstd[:]), ALU.mult)

            def update(s, k, l, gate):
                for src, dst, c in pieces(s, x[:, k, :]):
                    last = dve.scalar_tensor_tensor(out=dst, in0=src, scalar=mod[:, l, gate + k, c:c + 1], in1=dst,
                                                    op0=ALU.mult, op1=ALU.add)
                return last

            def out_proj(l):
                norm = 2 * l + 1
                if l == 0:
                    for n, k in enumerate(MIX_ORDER[l]):
                        low_part(k, mix[:, k, :], H_MIX[l], n, TOK)
                else:
                    dve.wait_ge(h_ready, H_MIX[l] + KT - 1)
                    low_part(KT - 1, mix[:, KT - 1, :], H_MIX[l], KT - 1, TOK)

                def updated(k):
                    s = (AT_OUT[l].items + k) % 2
                    if k in (0, 3):
                        dve.wait_ge(x_back[k // 3], 16 * (l + 1))
                    dve.wait_ge(unit_done, AT_OUT[l].units + k + 1)
                    update(s, k, l, G1).then_inc(read_out[s], 1)

                for k in range(KT - 1):
                    updated(k)
                    if k == 0:
                        gains(norm, FIRST_BATCHES + HEADS + GROUPS * l)
                    if k > 1:
                        add_square(norm, k - 1)
                add_square(norm, KT - 2)
                for k in range(KT):
                    low_part(k, gained(norm, k)[:], H_NORM[norm], k)
                    if k == 1:
                        updated(KT - 1)
                    if k == KT - 2:
                        add_square(norm, KT - 1)
                reciprocals(norm)

            def mlp(l):
                I, U, M = AT_MLP[l].items, AT_MLP[l].units, AT_MLP[l].minis
                norm = 2 * l + 2

                def group(g, last):
                    if l == 0:
                        steps.enter(None if last else g, 14 * GRP_MODS)
                    for j in range(GRP):
                        tile = l * GRP * GROUPS + j
                        chunks = BANKS * tile
                        s = (I + j) % 2
                        dve.wait_ge(unit_done, at(g, GRP_UNITS, U + j + 1))
                        dve.wait_ge(hid_ready, at(g, BANKS * GRP, chunks + 1))
                        dve.tensor_copy(bias[:, j, :], psum[:, s, BANKS - 1, CH:CH + 2])
                        for c in range(BANKS):
                            t = slice(c * CH, (c + 1) * CH)
                            dve.tensor_tensor(relu[:, t], psum[:, s, c, 0:CH], rstd[:, t], ALU.mult).then_inc(
                                scaled if c < BANKS - 1 else read_out[s], 1)
                        for c in range(BANKS):
                            t = slice(c * CH, (c + 1) * CH)
                            dve.wait_ge(relu_ready, at(g, BANKS * GRP, chunks + c + 1))
                            dve.tensor_tensor(relu2[:, t], relu[:, t], relu[:, t], ALU.mult).then_inc(relu2_ready, 1)
                        for c in range(BANKS):
                            t = slice(c * CH, (c + 1) * CH)
                            dve.wait_ge(hid_part_hi, at(g, BANKS * GRP, chunks + c + 1))
                            dve.tensor_tensor(hid_lo[:, j, t], relu2[:, t], hid_hi[:, j, t].bitcast(F32),
                                              ALU.subtract).then_inc(hid_ready, 1)
                        if l == 0:
                            sum_mod(g, GRP_MODS, MODS + j)
                    for k in range(2 * GRP):
                        s = (I + GRP + k) % 2
                        if k % 2 == 0:
                            dve.wait_ge(mini_done, at(g, GRP_MINIS, M + k // 2 + 1))
                        else:
                            dve.wait_ge(unit_done, at(g, GRP_UNITS, U + GRP + k // 2 + 1))
                        update(s, k, l, G2).then_inc(read_out[s], 1)
                        if l == 0 and k in (1, 3):
                            sum_mod(g, GRP_MODS, MODS + GRP + k // 2)
                        if last and k and l == 0:
                            low_part(k - 1, gained(norm, k - 1)[:], H_NORM[norm], k - 1)
                        if last and k > 1:
                            add_square(norm, k - 1)
                        if last and k == 0 and l == 0:
                            gains_early()
                    if l == 0:
                        steps.leave(1 if last else GROUPS - 1)
                        mods_out(1, g * GRP_MODS, GRP_MODS, at(g, GRP_MODS, MODS + GRP_MODS))

                def gains_early():
                    gains(norm, FIRST_BATCHES + HEADS + 3)

                with dve.Fori(0, GROUPS - 1) as g:
                    group(g, False)
                group(GROUPS - 1, True)
                if l == 0:
                    low_part(KT - 1, gained(norm, KT - 1)[:], H_NORM[norm], KT - 1)
                add_square(norm, KT - 1)
                if l == 0:
                    reciprocals(norm)

            def first_rows_out(item, n):
                dve.wait_ge(mini_done, item + 1)
                dve.tensor_copy(mod_rows[0:2, n, :].rearrange("p (b t) -> p b t", b=2), psum[0:2, item % 2, 0:2, :]).then_inc(read_out[item % 2], 1)

            first_rows_out(SCALE_ITEM, 0)
            mods_out(0, SC1, KT, KT)
            gains(0, 1)
            for k in range(KT):
                dve.wait_ge(gained_ready, k + 1)
                dve.tensor_copy(h_hi[:, k, 0:TOK], gained(0, k)[:, 0:TOK]).then_inc(part_hi, 1)
                low_part(k, gained(0, k)[:, 0:TOK], 0, k, TOK)
                if k == KT - 2:
                    first_rows_out(SHIFT_ITEM, 1)
            mods_out(0, SH1, KT, FIRST_MODS)
            dve.wait_ge(mod_read, FIRST_BATCHES)
            dve.tensor_copy(h_hi[:, :, TOK:COLS], mod[:, 0, SH1:SH1 + KT, :]).then_inc(dve_step, 1)
            after(steps.done())
            dve.tensor_tensor(h_lo[:, :, TOK:COLS], mod[:, 0, SH1:SH1 + KT, :], h_hi[:, :, TOK:COLS].bitcast(F32),
                              ALU.subtract).then_inc(shift_ready, 1)
            dve.wait_ge(powers_ready, 1)
            for d, m in enumerate((C_MF, C_MB)):
                dve.tensor_tensor(exps[:, d], exps[:, d], consts[:, m:m + P].unsqueeze(1).to_broadcast([P, HEADS, P]),
                                  ALU.mult).then_inc(dve_step, 1)
                masked = steps.done()
            after(masked)
            dve.tensor_tensor(mask[:], exps[:, 0], exps[:, 1], ALU.add).then_inc(powers_used, 1)

            reciprocals(0)

            I0, U0, M0 = AT_MIX[0].items, AT_MIX[0].units, AT_MIX[0].minis
            with dve.Fori(0, HEADS) as h:
                steps.enter(h, 41 + 14 * HEAD_MODS)

                def unit(n):
                    dve.wait_ge(unit_done, at(h, HEAD_UNITS, U0 + n + 1))

                def mini(n):
                    dve.wait_ge(mini_done, at(h, HEAD_MINIS, M0 + n + 1))

                def next_mod(n):
                    sum_mod(h, HEAD_MODS, FIRST_MODS + n)

                def rotate(dst):
                    dve.tensor_tensor(dst[:, 0:LAT], turned[:, 0:LAT], rope[:, 0, :], ALU.mult).then_inc(dve_step, 1)
                    steps.done()
                    dve.tensor_tensor(swapped[:, 0:LAT], swapped[:, 0:LAT], rope[:, 1, :], ALU.mult).then_inc(dve_step, 1)
                    after(steps.done())
                    dve.tensor_tensor(dst[:, 0:LAT], dst[:, 0:LAT], swapped[:, 0:LAT], ALU.add).then_inc(dve_step, 1)
                    steps.done()
                    return dve.tensor_copy(dst[:, LAT:TOK], turned[:, LAT:TOK])

                def by_chunk(t):
                    return t.rearrange("p (n t) -> p n t", t=P)

                def rows(t):
                    return t[:].rearrange("p (c n t) -> p c n t", c=BANKS, t=P)

                def all_rows(t):
                    return tile_of(t, h).unsqueeze(1).unsqueeze(1).to_broadcast([P, BANKS, BANKS, P])

                unit(0)
                s = I0 % 2
                scale_out(s, 0, turned, float(P) ** -0.5).then_inc(read_out[s], 1)
                next_mod(0)
                dve.wait_ge(rope_landed, 16)
                dve.wait_ge(projected, h * 2 + 1)
                rotate(kT).then_inc(k_ready, 1)
                unit(1)
                s = (I0 + 1) % 2
                scale_out(s, 1, v_raw).then_inc(read_out[s], 1)
                mini(0)
                s = (I0 + 2) % 2
                dve.wait_ge(state_out, h * 32 + 32)
                dve.wait_ge(gm_out, h + 1)
                dve.tensor_scalar(by_bank(k_fwd[:]), whole(s), col(k_dec[:, 0, :], h), None, ALU.mult)
                dve.tensor_scalar(by_bank(k_bwd[:]), whole(s), col(k_dec[:, 1, :], h), None, ALU.mult).then_inc(read_out[s], 1)
                next_mod(1)
                next_mod(2)
                unit(2)
                dve.wait_ge(k_ready, h + 1)
                s = (I0 + 3) % 2
                scale_out(s, 2, turned).then_inc(read_out[s], 1)
                next_mod(3)
                dve.wait_ge(projected, h * 2 + 2)
                rotate(qT).then_inc(dve_step, 1)
                after(steps.done())
                dve.wait_ge(q_dec_ready, h + 1)
                for d, t in enumerate((turned, swapped)):
                    last = dve.tensor_tensor(by_chunk(t[:, 0:LAT]), by_chunk(qT[:, 0:LAT]),
                                             q_dec[:, d, :].unsqueeze(1).to_broadcast([P, LCH, P]), ALU.mult)
                last.then_inc(q_ready, 1)
                unit(3)
                s = (I0 + 5) % 2
                scale_out(s, 3, v_raw).then_inc(read_out[s], 1)
                mini(2)
                dve.wait_ge(state_in, h * 32 + 32)
                s = (I0 + 6) % 2
                dve.tensor_copy(chunk(s_bwd, LCH), part(s, LCH)).then_inc(dve_step, 1)
                steps.done()
                for n in range(LCH - 1, 0, -1):
                    last = dve.scalar_tensor_tensor(out=chunk(s_bwd, n - 1), in0=chunk(s_bwd, n), scalar=col(g_chunk[:, 1, :], h),
                                                    in1=part(s, n), op0=ALU.mult, op1=ALU.add)
                    if n > 1:
                        last.then_inc(dve_step, 1)
                        after(steps.done())
                last.then_inc(read_out[s], 1)
                mini(3)
                s = (I0 + 7) % 2
                dve.tensor_tensor(rows(probs), whole(s).rearrange("p c (n t) -> p c n t", t=P), all_rows(mask),
                                  ALU.mult).then_inc(read_out[s], 1)
                mini(4)
                s = (I0 + 8) % 2
                dve.tensor_copy(chunk(k_bwd, LCH), part(s, LCH)).then_inc(dve_step, 1)
                steps.done()
                for n in range(LCH - 1):
                    last = dve.scalar_tensor_tensor(out=chunk(k_bwd, n + 1), in0=s0_fwd[:] if n == 0 else chunk(k_bwd, n),
                                                    scalar=col(g_chunk[:, 0, :], h), in1=part(s, n), op0=ALU.mult, op1=ALU.add)
                    if n < LCH - 2:
                        last.then_inc(dve_step, 1)
                        after(steps.done())
                last.then_inc(read_out[s], 1)
                next_mod(4)
                unit(4)
                s = (I0 + 9) % 2
                scale_out(s, 4, kT).then_inc(read_out[s], 1)
                next_mod(5)
                mini(6)
                s = (I0 + 11) % 2
                dve.tensor_copy(by_bank(v_raw[:]), whole(s)).then_inc(read_out[s], 1)
                item_out(dve, h, HEAD_ITEMS, I0 + 11)
                for n in range(NCH):
                    dve.bn_stats(stats[:, n, :], chunk(v_raw, n)).then_inc(dve_step, 1)
                    done = steps.done()
                after(done)
                dve.sem_inc(passed, 1)
                for n in range(NCH):
                    last = dve.bn_aggr(mean_var[:, n, :], stats[:, n, :])
                last.then_inc(o_var, 1)
                dve.wait_ge(o_var, h + 1)
                dve.wait_ge(o_root, h + 1)
                dve.reciprocal(row_rstd[:], row_rstd[:]).then_inc(dve_step, 1)
                after(steps.done())
                for n in range(NCH):
                    dve.tensor_scalar(chunk(v_raw, n), chunk(v_raw, n), mean_var[:, n, 0:1], row_rstd[:, n:n + 1],
                                      ALU.subtract, ALU.mult).then_inc(dve_step, 1)
                    done = steps.done()
                after(done)
                item_out(dve, h, HEAD_ITEMS, I0 + 10)
                dve.tensor_tensor(v_raw[:], v_raw[:], qT[:], ALU.mult).then_inc(o_ready, 1)
                dve.wait_ge(vf_root, h + 1)
                dve.reciprocal(vf_rstd[:], vf_rstd[:]).then_inc(dve_step, 1)
                after(steps.done())
                dve.tensor_tensor(by_chunk(kT[:]), by_chunk(kT[:]), vf_rstd[:].unsqueeze(2).to_broadcast([P, NCH, P]),
                                  ALU.mult).then_inc(vf_ready, 1)
                next_mod(6)
                unit(5)
                s = (I0 + 13) % 2
                scale_out(s, 5, k_fwd).then_inc(read_out[s], 1)
                next_mod(7)
                mini(9)
                s = (I0 + 15) % 2
                dve.tensor_tensor(rows(probs), whole(s).rearrange("p c (n t) -> p c n t", t=P), all_rows(bs_all),
                                  ALU.add).then_inc(read_out[s], 1)
                item_out(dve, h, HEAD_ITEMS, I0 + 15)
                dve.wait_ge(x_spilled, 16)
                dve.wait_ge(activated, at(h, HEAD_UNITS, HEAD_UNITS))
                dve.tensor_tensor(tile_of(mix, h + HEADS), probs[:], k_fwd[:], ALU.mult).then_inc(gm_out, 1)
                mods_out(0, h * HEAD_MODS + FIRST_MODS, HEAD_MODS, at(h, HEAD_MODS, FIRST_MODS + HEAD_MODS))
            steps.leave(HEADS)
            out_proj(0)
            mlp(0)

            I0, U0 = AT_MIX[1].items, AT_MIX[1].units
            dve.memset(xin[:, 0:LPAD], 0.0)
            dve.memset(xin[:, LPAD + LAT:CTX0 + LPAD], 0.0)
            dve.memset(xin[:, CTX0 + LPAD + CTX:], 0.0).then_inc(xc_ready, 1)
            runs = ((0, LAT, 0), (LAT, TOK, CTX0))

            def convolution(i, n):
                b = n if i is None else i + n
                dve.wait_ge(unit_done, at(i, BLK_UNITS, U0 + n * BLK_UNITS + 1))
                dve.wait_ge(xc_ready, b + 1)
                s = I0 % 2
                dve.tensor_copy(bias[:, 0, :], psum[:, s, BANKS - 1, CH:CH + 2])
                dve.tensor_tensor(xin[:, LPAD:LPAD + LATC * CH].rearrange("p (c t) -> p c t", c=LATC), psum[:, s, 0:LATC, 0:CH],
                                  rstd[:, 0:LATC * CH].rearrange("p (c t) -> p c t", c=LATC), ALU.mult)
                dve.tensor_tensor(xin[:, LPAD + LATC * CH:LPAD + LAT], psum[:, s, LATC, 0:LREST], rstd[:, LATC * CH:LAT], ALU.mult)
                dve.tensor_tensor(xin[:, CTX0 + LPAD:CTX0 + LPAD + CTX], psum[:, s, LATC, LREST:CH], rstd[:, LAT:TOK],
                                  ALU.mult).then_inc(read_out[s], 1)
                dve.wait_ge(xin_ready, b + 1)
                if n:
                    dve.wait_ge(gated_ready, at(i, 2, 2 * n))
                for j in range(4):
                    for start, end, row in runs:
                        src, w = xin[:, row + j:row + j + end - start], col(par, b + (R_CONVW + j * KT))
                        if j == 0:
                            last = dve.tensor_scalar(xc[:, start:end], src, w, col(par, b + R_CONVB), ALU.mult, ALU.add)
                        else:
                            last = dve.scalar_tensor_tensor(out=xc[:, start:end], in0=src, scalar=w, in1=xc[:, start:end],
                                                            op0=ALU.mult, op1=ALU.add)
                        if j < 3:
                            last.then_inc(dve_step, 1)
                            done = steps.done()
                    if j < 3:
                        after(done)
                last.then_inc(xc_ready, 1)

            def output_gate(i, n):
                dve.wait_ge(unit_done, at(i, BLK_UNITS, U0 + n * BLK_UNITS + 2))
                if n:
                    dve.wait_ge(gelu_ready, at(i, 1, n))
                s = (I0 + 1) % 2
                scale_out(s, 1, gate_raw).then_inc(read_out[s], 1)

            def lru_block(b, last_block):
                steps.enter(None if last_block else b, 10 if last_block else 16)
                if last_block:
                    dve.wait_ge(lru_done, KT)
                    for k in range(KT - 1):
                        dve.tensor_copy(h_hi[:, k, 0:TOK], mix[:, k, :]).then_inc(part_hi, 1)
                        if k < DVE_LOW:
                            low_part(k, mix[:, k, :], H_MIX[1], k, TOK)
                for d in range(2):
                    dve.wait_ge(tanh_ready, at(b, 2, d + 1))
                    dve.scalar_tensor_tensor(out=work[d][:], in0=work[d][:], scalar=1.0, in1=rate[d][:],
                                             op0=ALU.add, op1=ALU.mult).then_inc(dve_step, 1)
                    after(steps.done())
                    dve.tensor_scalar(rate[d][:], work[d][:], -1.0, 1.0, ALU.mult, ALU.add).then_inc(dve_step, 1)
                    after(steps.done())
                    dve.scalar_tensor_tensor(out=work[d][:], in0=work[d][:], scalar=2.0, in1=work[d][:],
                                             op0=ALU.subtract, op1=ALU.mult).then_inc(under_root, 1)
                if not last_block:
                    convolution(b, 1)
                for d in range(2):
                    dve.wait_ge(root_ready, at(b, 2, d + 1))
                    dve.wait_ge(gated_ready, at(b, 2, d + 1))
                    dve.tensor_tensor(gated[d][:], work[d][:], gated[d][:], ALU.mult).then_inc(dve_step, 1)
                    multiplied = steps.done()
                    if d == 0 and not last_block:
                        output_gate(b, 1)
                    after(multiplied)
                    for start, end, _row in runs:
                        step = 1 if d == 0 else -1
                        first = col(par, b + (R_LF, R_LB)[d]) if start == 0 else 0.0
                        last = dve.tensor_tensor_scan(work[d][:, start:end][:, ::step], rate[d][:, start:end][:, ::step],
                                                      gated[d][:, start:end][:, ::step], first, ALU.mult, ALU.add)
                        if start == 0:
                            last.then_inc(dve_step, 1)
                            steps.done()
                    last.then_inc(scanned, 1)
                dve.wait_ge(scanned, at(b, 2, 4))
                dve.tensor_copy(col(lru_last[:, 0, :], b), work[0][:, TOK - 1:TOK])
                dve.tensor_copy(col(lru_last[:, 1, :], b), work[1][:, LAT:LAT + 1]).then_inc(dve_step, 1)
                after(steps.done())
                dve.tensor_tensor(work[1][:], work[1][:], work[0][:], ALU.add).then_inc(dve_step, 1)
                after(steps.done())
                dve.wait_ge(gelu_ready, b + 1)
                dve.tensor_tensor(tile_of(mix, b), work[1][:], gelu_gate[:], ALU.mult).then_inc(lru_done, 1)
                steps.leave(1 if last_block else KT - 1)

            convolution(None, 0)
            output_gate(None, 0)
            dve.wait_ge(x_spilled, 32)
            with dve.Fori(0, KT - 1) as b:
                lru_block(b, False)
            lru_block(KT - 1, True)
            out_proj(1)
            mlp(1)
            dve.wait_ge(ssq_read, BANKS * 4 + 1)
            dve.reciprocal(y_rstd[:], y_rstd[:]).then_inc(y_rstd_ready, 1)
            dve.wait_ge(y_rstd_ready, 1)
            for n in range(1, NCH, 2):
                s = (AT_END.items + n) % 2
                dve.wait_ge(mini_done, AT_END.minis + n + 1)
                dve.tensor_scalar(y_rows[:, n, :].rearrange("p (k t) -> p k t", k=KT),
                                  psum[:, s, 0:2, :].rearrange("p b (k t) -> p (b k) t", k=4), y_rstd[:, n:n + 1], None,
                                  ALU.mult).then_inc(read_out[s], 1)


def constants():
    i = np.arange(P, dtype=np.float64)
    ahead = i[None, :] - i[:, None]
    table = np.zeros((P, C_ALL), np.float32)
    for at, block in ((C_ID, np.eye(P)), (C_DF, np.maximum(ahead, 0)), (C_DB, np.maximum(-ahead - 1, 0)),
                      (C_MF, ahead >= 0), (C_MB, ahead < 0),
                      (C_QF, np.broadcast_to(i + 1, (P, P))), (C_QB, np.broadcast_to(P - 1 - i, (P, P)))):
        table[:, at:at + P] = block
    table[:, C_KF], table[:, C_KB] = P - 1 - i, i
    pos = np.arange(LAT)
    half = P // 2
    freq = (np.float32(ROPE_BASE) ** (-np.arange(half // 2, dtype=np.float32) / np.float32(half // 2))).astype(np.float32)
    turns = np.zeros((P, 2, LAT), np.float32)
    for part, p in enumerate((pos // GRID_W, pos % GRID_W)):
        angle = (p.astype(np.float32)[None, :] * freq[:, None]).astype(np.float64)
        for side, sign in enumerate((-1.0, 1.0)):
            rows = slice(part * half + side * half // 2, part * half + (side + 1) * half // 2)
            turns[rows, 0], turns[rows, 1] = np.cos(angle), sign * np.sin(angle)
    return table, turns


_INS = ['x_prompt', 'x_sample', 'c', 'c_ctx', 'state_ret_fwd', 'state_ret_bwd', 'state_lru_fwd', 'state_lru_bwd',
        'mod_w', 'mod_b', 'norm_mix', 'norm_mlp', 'mlp_w1', 'mlp_w2', 'ab_w_in', 'ab_w_out', 'ret_decay_fwd',
        'ret_decay_bwd', 'gmlp_ws', 'gmlp_bs', 'lru_w_in', 'lru_conv_w', 'lru_conv_b', 'lru_gate_a_w', 'lru_gate_a_b',
        'lru_gate_x_w', 'lru_gate_x_b', 'lru_lambda', 'lru_w_out', 'final_norm']
_OUTS = [('y_prompt', (1, CTX, D_MODEL)), ('y_sample', (1, LAT, D_MODEL)), ('new_ret_fwd', (1, 1, HEADS, P, P)),
         ('new_ret_bwd', (1, 1, HEADS, P, P)), ('new_lru_fwd', (1, 1, D_MODEL)), ('new_lru_bwd', (1, 1, D_MODEL))]


def kernel(**inputs):
    import concourse.bacc as bacc
    from concourse.bass_utils import run_bass_kernel_spmd as run

    nc = bacc.Bacc("TRN2", target_bir_lowering=False, num_devices=1)
    arrays, args = {}, {}
    named = {name: np.ascontiguousarray(inputs[name]) for name in _INS}
    named['consts'], named['rope'] = constants()
    for name, value in named.items():
        arrays[f"in_{name}"] = value
        args[name] = nc.dram_tensor(f"in_{name}", value.shape, F32, kind="ExternalInput").ap()
    for name, shape in _OUTS:
        args[name] = nc.dram_tensor(f"out_{name}", shape, F32, kind="ExternalOutput").ap()
    with nc.allow_non_contiguous_dma(reason="final states of the RG-LRU lie by columns"):
        build(nc, args)
    r = run(nc, [arrays], core_ids=[0])
    return tuple(r.results[0][f"out_{name}"] for name, _ in _OUTS)
```
